# Optimizing a Trainium2 kernel written in Bass

```python
import jax, jax.numpy as jnp
from jax import lax
import numpy as np

D_MODEL = 1024
BATCH = 1
SEQ = 1024
DEPTH = 2

CHUNK = 64
ROPE_THETA = 10000.0
NORM_EPS = 1e-6
M_HEADS = 4
M_DQK = 64
M_DV = 128
CONV_K = 4
S_QHEADS = 8
S_KVHEADS = 2
S_HD = 64
S_WINDOW = 128
C_HEADS = 8
C_Q_LORA = 384
C_KV_LORA = 256
C_NOPE = 128
C_ROPE = 64
C_DV = 128
Q_BLOCK = 128

M_QK_W = M_HEADS * M_DQK
M_V_W = M_HEADS * M_DV
S_Q_W = S_QHEADS * S_HD
S_KV_W = S_KVHEADS * S_HD
MIX_EVEN = M_V_W + S_Q_W
MIX_ODD = C_HEADS * C_DV
EVEN_WIDTHS = (M_QK_W, M_QK_W, M_V_W, M_V_W, 2 * M_HEADS, S_Q_W, S_KV_W, S_KV_W, MIX_EVEN)
E_IN = sum(EVEN_WIDTHS)
ODD_WIDTHS = (C_Q_LORA, C_KV_LORA, C_ROPE, MIX_ODD)
O_IN = sum(ODD_WIDTHS)
N_EVEN = (DEPTH + 1) // 2
N_ODD = DEPTH // 2

kernel_name = "hybrid_mlstm_swa_mla_stream"

def rms_norm(x, g):
    xf = x.astype(jnp.float32)
    y = xf * lax.rsqrt(jnp.mean(xf * xf, axis=-1, keepdims=True) + NORM_EPS)
    return (y * g.astype(jnp.float32)).astype(x.dtype)

def split_cols(x, widths):
    return jnp.split(x, np.cumsum(widths)[:-1].tolist(), axis=-1)

def rope_cos_sin(seq_len, dim):
    inv = 1.0 / (ROPE_THETA ** (jnp.arange(0, dim, 2, dtype=jnp.float32) / dim))
    ang = jnp.arange(seq_len, dtype=jnp.float32)[:, None] * inv[None, :]
    return jnp.cos(ang), jnp.sin(ang)

def apply_rope(x, cos, sin):
    half = x.shape[-1] // 2
    x1 = x[..., :half].astype(jnp.float32)
    x2 = x[..., half:].astype(jnp.float32)
    c = cos[None, :, None, :]
    s = sin[None, :, None, :]
    return jnp.concatenate([x1 * c - x2 * s, x2 * c + x1 * s], axis=-1).astype(x.dtype)

def causal_conv(x, w):
    S = x.shape[1]
    K = w.shape[0]
    xp = jnp.pad(x, ((0, 0), (K - 1, 0), (0, 0)))
    out = w[0] * xp[:, 0:S]
    for tap in range(1, K):
        out = out + w[tap] * xp[:, tap:tap + S]
    return out

def mlstm_chunkwise(q, k, v, i_pre, f_pre):
    B, S, H, dk = q.shape
    dv = v.shape[-1]
    L = CHUNK
    nC = S // L
    f32 = jnp.float32

    def to_chunks(t):
        return t.astype(f32).reshape(B, nC, L, H, -1).transpose(1, 0, 3, 2, 4)

    qc, kc, vc = to_chunks(q), to_chunks(k), to_chunks(v)
    li = i_pre.astype(f32).reshape(B, nC, L, H).transpose(1, 0, 3, 2)
    lf = jax.nn.log_sigmoid(f_pre.astype(f32)).reshape(B, nC, L, H).transpose(1, 0, 3, 2)
    causal = jnp.tril(jnp.ones((L, L), dtype=bool))

    def step(carry, inp):
        C, n, m = carry
        qt, kt, vt, lit, lft = inp
        b = jnp.cumsum(lft, axis=-1)
        dlog = jnp.where(causal, b[..., :, None] - b[..., None, :] + lit[..., None, :], -jnp.inf)
        inter_log = b + m[..., None]
        m_t = jnp.maximum(inter_log, jnp.max(dlog, axis=-1))
        w_intra = jnp.exp(dlog - m_t[..., None])
        w_inter = jnp.exp(inter_log - m_t)
        s = jnp.einsum('bhtd,bhsd->bhts', qt, kt) * w_intra
        num = jnp.einsum('bhts,bhsv->bhtv', s, vt) + w_inter[..., None] * jnp.einsum('bhvd,bhtd->bhtv', C, qt)
        den = jnp.sum(s, axis=-1) + w_inter * jnp.einsum('bhd,bhtd->bht', n, qt)
        h = num / jnp.maximum(jnp.abs(den), jnp.exp(-m_t))[..., None]
        b_last = b[..., -1]
        w_log = b_last[..., None] - b + lit
        m_new = jnp.maximum(b_last + m, jnp.max(w_log, axis=-1))
        decay = jnp.exp(b_last + m - m_new)
        w_state = jnp.exp(w_log - m_new[..., None])
        C = decay[..., None, None] * C + jnp.einsum('bhs,bhsv,bhsd->bhvd', w_state, vt, kt)
        n = decay[..., None] * n + jnp.einsum('bhs,bhsd->bhd', w_state, kt)
        return (C, n, m_new), h

    init = (jnp.zeros((B, H, dv, dk), f32), jnp.zeros((B, H, dk), f32), jnp.zeros((B, H), f32))
    _, hs = lax.scan(step, init, (qc, kc, vc, li, lf))
    return hs.transpose(1, 0, 3, 2, 4).reshape(B, S, H, dv)

def swa_with_sinks(q, k, v, sinks):
    B, S, HQ, d = q.shape
    HKV = k.shape[2]
    G = HQ // HKV
    L = CHUNK
    nC = S // L
    W = S_WINDOW // CHUNK
    qc = q.reshape(B, nC, L, HKV, G, d)
    kc = k.reshape(B, nC, L, HKV, d)
    vc = v.reshape(B, nC, L, HKV, d)

    def band(t):
        parts = [jnp.pad(t, ((0, 0), (j, 0), (0, 0), (0, 0), (0, 0)))[:, :nC] for j in range(W - 1, -1, -1)]
        return jnp.concatenate(parts, axis=2)

    kb, vb = band(kc), band(vc)
    key_offset = jnp.repeat(jnp.arange(W - 1, -1, -1), L)[None, :]
    valid = (jnp.arange(nC)[:, None] - key_offset) >= 0
    scores = jnp.einsum('bcqhgd,bckhd->bchgqk', qc, kb).astype(jnp.float32) * (d ** -0.5)
    scores = jnp.where(valid[None, :, None, None, None, :], scores, -jnp.inf)
    sink = jnp.broadcast_to(sinks.astype(jnp.float32).reshape(1, 1, HKV, G, 1, 1), scores.shape[:-1] + (1,))
    probs = jax.nn.softmax(jnp.concatenate([scores, sink], axis=-1), axis=-1)[..., :-1]
    out = jnp.einsum('bchgqk,bckhd->bcqhgd', probs.astype(v.dtype), vb)
    return out.reshape(B, S, HQ * d)

def block_causal_attention(q, k, v):
    B, S, H, dq = q.shape
    dv = v.shape[-1]
    nQB = S // Q_BLOCK
    scale = dq ** -0.5
    key_chunk = jnp.arange(S) // CHUNK
    qb = q.reshape(B, nQB, Q_BLOCK, H, dq).transpose(1, 0, 2, 3, 4)

    def one_block(args):
        q_blk, blk = args
        q_chunk = (blk * Q_BLOCK + jnp.arange(Q_BLOCK)) // CHUNK
        s = jnp.einsum('bqhd,bkhd->bhqk', q_blk, k).astype(jnp.float32) * scale
        s = jnp.where((key_chunk[None, :] <= q_chunk[:, None])[None, None], s, -jnp.inf)
        p = jax.nn.softmax(s, axis=-1).astype(v.dtype)
        return jnp.einsum('bhqk,bkhd->bqhd', p, v)

    out = lax.map(one_block, (qb, jnp.arange(nQB)))
    return out.transpose(1, 0, 2, 3, 4).reshape(B, S, H * dv)

def even_mixer(h, w_in, conv_w, gate_b, head_g, sinks, w_out, cos, sin):
    B, S, _ = h.shape
    q_m, k_m, v_m, o_m, if_m, q_s, k_s, v_s, z = split_cols(h @ w_in, EVEN_WIDTHS)
    qk = jax.nn.silu(causal_conv(jnp.concatenate([q_m, k_m], axis=-1), conv_w))
    q_m, k_m = jnp.split(qk, 2, axis=-1)
    q_m = q_m.reshape(B, S, M_HEADS, M_DQK)
    k_m = k_m.reshape(B, S, M_HEADS, M_DQK) * (M_DQK ** -0.5)
    v_m = v_m.reshape(B, S, M_HEADS, M_DV)
    gates = if_m + gate_b
    h_m = mlstm_chunkwise(q_m, k_m, v_m, gates[..., :M_HEADS], gates[..., M_HEADS:])
    h_m = rms_norm(h_m, head_g.reshape(M_HEADS, M_DV)).reshape(B, S, M_V_W).astype(h.dtype)
    h_m = h_m * jax.nn.sigmoid(o_m)
    q_s = apply_rope(q_s.reshape(B, S, S_QHEADS, S_HD), cos, sin)
    k_s = apply_rope(k_s.reshape(B, S, S_KVHEADS, S_HD), cos, sin)
    v_s = v_s.reshape(B, S, S_KVHEADS, S_HD)
    h_s = swa_with_sinks(q_s, k_s, v_s, sinks)
    y = jnp.concatenate([h_m, h_s], axis=-1) * jax.nn.silu(z)
    return y @ w_out

def odd_mixer(h, w_in, q_g, kv_g, w_uq, w_ukv, w_out, cos, sin):
    B, S, _ = h.shape
    cq, ckv, kr, z = split_cols(h @ w_in, ODD_WIDTHS)
    q = (rms_norm(cq, q_g) @ w_uq).reshape(B, S, C_HEADS, C_NOPE + C_ROPE)
    kv = (rms_norm(ckv, kv_g) @ w_ukv).reshape(B, S, C_HEADS, C_NOPE + C_DV)
    q = jnp.concatenate([q[..., :C_NOPE], apply_rope(q[..., C_NOPE:], cos, sin)], axis=-1)
    k_rope = apply_rope(kr.reshape(B, S, 1, C_ROPE), cos, sin)
    k = jnp.concatenate([kv[..., :C_NOPE], jnp.broadcast_to(k_rope, (B, S, C_HEADS, C_ROPE))], axis=-1)
    v = kv[..., C_NOPE:]
    o = block_causal_attention(q, k, v)
    return (o * jax.nn.silu(z)) @ w_out

def setup_inputs(seed: int = 0) -> dict:
    key = jax.random.key(seed)
    ks = jax.random.split(key, 20)
    nrm = jax.random.normal
    D = D_MODEL
    f_bias = 3.0 + 0.5 * nrm(ks[6], (N_EVEN, M_HEADS))
    i_bias = 0.1 * nrm(ks[7], (N_EVEN, M_HEADS))
    return {
        'x': nrm(ks[0], (BATCH, SEQ, D)),
        'c': nrm(ks[1], (BATCH, D)),
        'ada_w': nrm(ks[2], (DEPTH, D, 3 * D)) * D ** -0.5,
        'ada_b': 0.02 * nrm(ks[3], (DEPTH, 3 * D)),
        'norm_g': 1.0 + 0.1 * nrm(ks[4], (DEPTH, D)),
        'e_w_in': nrm(ks[5], (N_EVEN, D, E_IN)) * D ** -0.5,
        'e_conv_w': nrm(ks[8], (N_EVEN, CONV_K, 2 * M_QK_W)) * CONV_K ** -0.5,
        'e_gate_b': jnp.concatenate([i_bias, f_bias], axis=-1),
        'e_head_g': 1.0 + 0.1 * nrm(ks[9], (N_EVEN, M_V_W)),
        'e_sinks': 0.5 * nrm(ks[10], (N_EVEN, S_QHEADS)),
        'e_w_out': nrm(ks[11], (N_EVEN, MIX_EVEN, D)) * MIX_EVEN ** -0.5,
        'o_w_in': nrm(ks[12], (N_ODD, D, O_IN)) * D ** -0.5,
        'o_q_g': 1.0 + 0.1 * nrm(ks[13], (N_ODD, C_Q_LORA)),
        'o_kv_g': 1.0 + 0.1 * nrm(ks[14], (N_ODD, C_KV_LORA)),
        'o_w_uq': nrm(ks[15], (N_ODD, C_Q_LORA, C_HEADS * (C_NOPE + C_ROPE))) * C_Q_LORA ** -0.5,
        'o_w_ukv': nrm(ks[16], (N_ODD, C_KV_LORA, C_HEADS * (C_NOPE + C_DV))) * C_KV_LORA ** -0.5,
        'o_w_out': nrm(ks[17], (N_ODD, MIX_ODD, D)) * MIX_ODD ** -0.5,
        'final_g': 1.0 + 0.1 * nrm(ks[18], (D,)),
    }

def reference(x, c, ada_w, ada_b, norm_g, e_w_in, e_conv_w, e_gate_b, e_head_g, e_sinks, e_w_out,
              o_w_in, o_q_g, o_kv_g, o_w_uq, o_w_ukv, o_w_out, final_g):
    S = x.shape[1]
    cos_s, sin_s = rope_cos_sin(S, S_HD)
    cos_c, sin_c = rope_cos_sin(S, C_ROPE)
    c_act = jax.nn.silu(c)
    for layer in range(DEPTH):
        mod = c_act @ ada_w[layer] + ada_b[layer]
        shift, scale, gate = jnp.split(mod, 3, axis=-1)
        h = rms_norm(x, norm_g[layer]) * (1.0 + scale[:, None, :]) + shift[:, None, :]
        j = layer // 2
        if layer % 2 == 0:
            y = even_mixer(h, e_w_in[j], e_conv_w[j], e_gate_b[j], e_head_g[j], e_sinks[j], e_w_out[j], cos_s, sin_s)
        else:
            y = odd_mixer(h, o_w_in[j], o_q_g[j], o_kv_g[j], o_w_uq[j], o_w_ukv[j], o_w_out[j], cos_c, sin_c)
        x = x + gate[:, None, :] * y
    return rms_norm(x, final_g)


_drawn_inputs = setup_inputs


def setup_inputs(seed=0):
    import zlib

    import numpy as np

    out = dict(_drawn_inputs(seed))
    spreads = {}
    factors = {'ada_b': 2.777, 'e_head_g': 2.852, 'e_sinks': 8.0, 'o_q_g': 8.0}
    for name, (base, spread) in spreads.items():
        noise = np.random.default_rng([zlib.crc32(name.encode()), seed]).standard_normal(out[name].shape)
        drawn = base * np.exp(spread * noise) if base else spread * noise
        out[name] = __import__('jax').numpy.asarray(drawn.astype(out[name].dtype))
    for name, factor in factors.items():
        out[name] = (out[name] * factor).astype(out[name].dtype)
    return out
```

```python
from contextlib import ExitStack

import concourse.bass as bass
from concourse import mybir

F32 = mybir.dt.float32
F32R = mybir.dt.float32r
BF16 = mybir.dt.bfloat16
I32 = mybir.dt.int32
ALU = mybir.AluOpType
ACT = mybir.ActivationFunctionType
AX = mybir.AxisListType.X

P = 128
S, D = 1024, 1024
T = S // P
KD = D // P
CW = 256
EPS = 1e-6
M_HEADS, M_DQK, M_DV, CONV_K = 4, 64, 128, 4
S_QH, S_KVH, S_HD = 8, 2, 64
S_G = S_QH // S_KVH
C_HEADS, C_QL, C_KVL, C_NOPE, C_ROPE, C_DV = 8, 384, 256, 128, 64, 128
KQ, KKV = C_QL // P, C_KVL // P
M_SCALE = M_DQK ** -0.5
S_SCALE = S_HD ** -0.5
C_SCALE = (C_NOPE + C_ROPE) ** -0.5
VW = M_DV + 2
E_Q, E_K, E_V, E_O, E_IF = 0, 256, 512, 1024, 1536
E_SQ, E_SK, E_SV, E_Z = 1544, 2056, 2184, 2312
O_CQ, O_CKV, O_KR, O_Z = 0, 384, 640, 704
CRW = 768
FLAT = 2112
NPSUM = 8
SPLITS = ("kTE", "aqTE", "apTE", "yTE", "qrTE", "pqTE", "pkTE", "pvE", "mpTE", "cTE")
ACT_KINDS = frozenset(("csilu", "ws", "xsq", "hx", "kvgE", "rowsB", "asm", "cols", "mqkE", "silu", "mvE", "vsp", "mBE",
                       "hsq", "moE", "zE", "latE", "lsq", "msm") + SPLITS)
DVE_KINDS = frozenset(("ones", "adaA", "adaE", "rs", "xh", "hx", "kvgE", "sqE", "pqE", "gTE", "rowsA", "rows", "asm",
                       "ano", "colsE", "cols", "conv", "qksp", "mSE", "kNE", "mOE", "mCE", "mfin", "mscale", "moE",
                       "zE", "poE", "lrs", "lsc", "msm", "mno", "fin") + SPLITS)


def chunks():
    c = {}
    c["kvg"] = [(0, KD, 264, [("e_in", E_SK, 128, 0), ("e_in", E_SV, 128, 128), ("e_in", E_IF, 8, 256)])]
    for g in range(2):
        c["sq", g] = [(0, KD, CW, [("e_in", E_SQ + CW * g, CW, 0)])]
    for p in range(2):
        c["mqk", p] = [(0, KD, CW, [("e_in", E_Q + P * p, P, 0), ("e_in", E_K + P * p, P, P)])]
        c["mv", p] = [(0, KD, CW, [("e_in", E_V + CW * p, CW, 0)])]
        c["mo", p] = [(0, KD, CW, [("e_in", E_O + CW * p, CW, 0)])]
    for z in range(4):
        c["z", 0, z] = [(0, KD, CW, [("e_in", E_Z + CW * z, CW, 0)])]
        c["z", 1, z] = [(0, KD, CW, [("o_in", O_Z + CW * z, CW, 0)])]
        c["out", 0, z] = [(0, KD, CW, [("e_out", CW * z, CW, 0)])]
        c["out", 1, z] = [(0, KD, CW, [("o_out", CW * z, CW, 0)])]
    c["lat", 0] = [(0, KD, CW, [("o_in", 0, CW, 0)])]
    c["lat", 1] = [(0, KD, CW, [("o_in", CW, CW, 0)])]
    c["lat", 2] = [(0, KD, 192, [("o_in", 2 * CW, 192, 0)])]
    c["uqr"] = [(0, KQ, 512, [("uq", 192 * h + C_NOPE, C_ROPE, C_ROPE * h) for h in range(C_HEADS)])]
    for a in range(C_HEADS // 2):
        c["hp", a] = [(0, KQ, 256, [("uq", 192 * (2 * a + j), P, P * j) for j in range(2)]),
                      (768, KKV, 512, [("ukv", 512 * a, 512, 0)])]
    return c


CHUNKS = chunks()
LAT_W = {0: CW, 1: CW, 2: 192}


def plan():
    o = []

    def chunk(name, steps, split_next_here=True):
        at = len(o)
        o.extend(steps)
        marks.append([name, at + 3])

    marks = []

    def ada(l, cs):
        cs = list(cs)
        for n, c in enumerate(cs):
            o.append(("adaA", l, c))
            if n:
                o.append(("adaE", l, cs[n - 1]))
            o.append(("adaM", l, c))
        o.append(("adaE", l, cs[-1]))

    def norm(l, half):
        for i in range(4 * half, 4 * half + 4):
            o.append(("xsq", l, i))
        o.append(("rs", l, half))
        for i in range(4 * half, 4 * half + 4):
            o.append(("xh", l, i))

    def hidden(l):
        for half in range(2):
            for k in range(KD):
                o.append(("xT", l, k, half))
                o.append(("hx", l, k, half))

    def proj(kind, *key, lag=1, evac=None):
        out = []
        for i in range(T + lag):
            if i < T:
                out.append((kind, *key, i))
            if i >= lag:
                out.append((evac or kind + "E", *key, i - lag))
        return out

    for i in range(T):
        o.append(("xl", 0, i))
    o += [("ones",), ("csilu",)]
    norm(0, 0)
    norm(0, 1)
    ada(0, range(8))
    hidden(0)
    chunk("kvg", proj("kvg"))
    for half in range(2):
        o += [("gT", half), ("gTE", half), ("kT", half), ("kTE", half)]
    chunk(("sq", 0), proj("sq", 0))
    o += [("rowsA",), ("rowsB",), ("rows",)]
    chunk(("sq", 1), proj("sq", 1))
    ada(0, range(8, 12))
    units = [(i, g, ap) for i in range(T) for g in range(2) for ap in range(2)]
    n = len(units)
    for u in range(n + 3):
        if u >= 3:
            o.append(("ano", *units[u - 3]))
        if u < n:
            i, g, ap = units[u]
            if g == 0 and ap == 0:
                o += [("aqT", i), ("aqTE", i)]
            o += [("asc", *units[u]), ("asm", *units[u])]
        if 1 <= u <= n:
            o += [("apT", *units[u - 1]), ("apTE", *units[u - 1])]
        if 2 <= u <= n + 1:
            o.append(("apv", *units[u - 2]))
        if u == n // 2:
            ada(1, range(0, 2))
    o += [("colsT",), ("colsE",), ("cols",)]
    for p in range(2):
        steps = []
        for which in range(2):
            for half in range(2):
                steps += [("mqk", p, which, half), ("mqkE", p, which, half)]
            steps += [("conv", p, which), ("silu", p, which), ("qksp", p, which)]
        chunk(("mqk", p), steps)
        chunk(("mv", p), proj("mv", p))
        ada(1, range(2 + 2 * p, 4 + 2 * p))
        for i in range(T + 1):
            if i < T:
                o += [("vsp", p, i), ("mB", p, i), ("mBE", p, i), ("mS", p, i)]
                if i < T - 1:
                    o.append(("kN", p, i))
                o.append(("mSE", p, i))
                if i < T - 1:
                    o.append(("kNE", p, i))
            if i >= 1:
                o += [("mOE", p, i - 1), ("hsq", p, i - 1)]
            if i < T:
                o.append(("mO", p, i))
                if i < T - 1:
                    o += [("mC", p, i), ("mCE", p, i)]
    o.append(("mfin",))
    for i in range(T):
        o.append(("mscale", i))
    for p in range(2):
        chunk(("mo", p), proj("mo", p))
        ada(1, range(6 + p, 7 + p))
    for z in range(4):
        chunk(("z", 0, z), proj("z", 0, z))

    def out_layer(l):
        for half in range(2):
            for k in range(KD):
                o.append(("yT", l, k, half))
                o.append(("yTE", l, k, half))
            for i in range(4 * half, 4 * half + 4):
                o.append(("xl", l + 2, i))
        for oc in range(4):
            chunk(("out", l, oc), proj("po", l, oc))

    out_layer(0)
    for i in range(T):
        o.append(("xs", i))
    norm(1, 0)
    norm(1, 1)
    hidden(1)
    for c in range(3):
        chunk(("lat", c), proj("lat", c))
        if c:
            ada(1, range(6 + 2 * c, 8 + 2 * c))
    for i in range(T):
        o.append(("lsq", i))
    for z in range(2):
        chunk(("z", 1, z), proj("z", 1, z))
    o.append(("lrs",))
    for i in range(T):
        o.append(("lsc", i))
    for z in range(2, 4):
        chunk(("z", 1, z), proj("z", 1, z))
    for k in range(6):
        for half in range(2):
            o += [("cT", k, half), ("cTE", k, half)]
    steps = []
    for s in proj("pq"):
        steps.append(s)
        if s[0] == "pqE":
            steps.append(("qs", s[1]))
    chunk("uqr", steps)
    head = {}
    for h in range(C_HEADS):
        pre = []
        if h % 2 == 0:
            pre.append(("ql", h // 2))
            for half in range(2):
                pre += [("qrT", h // 2, half), ("qrTE", h // 2, half)]
        for what in ("pqT", "pkT"):
            for half in range(2):
                pre += [(what, h, half), (what + "E", h, half)]
        head[h] = pre
    units = [(h, i) for h in range(C_HEADS) for i in range(T)]
    n = len(units)
    for u in range(n + 3):
        if u >= 3:
            o.append(("mno", *units[u - 3]))
        if u < n:
            h, i = units[u]
            if i == 0:
                if h % 2 == 0:
                    chunk(("hp", h // 2), head[h])
                else:
                    o.extend(head[h])
            o += [("msc", h, i, b) for b in range(i // 4 + 1)]
            o.append(("msm", h, i))
            if h % 2 == 0 and i == 4:
                marks[-1][1] = len(o)
        if 2 <= u <= n + 1:
            h, i = units[u - 2]
            o += [("mpv", h, i, b) for b in range(i // 4 + 1)]
        if 1 <= u <= n:
            h, i = units[u - 1]
            if i == 0:
                for half in range(2):
                    o += [("pv", h, half), ("pvE", h, half)]
            for b in range(i // 4 + 1):
                o += [("mpT", h, i, b), ("mpTE", h, i, b)]
    out_layer(1)
    o.append(("fg",))
    for half in range(2):
        for i in range(4 * half, 4 * half + 4):
            o.append(("xsq", 2, i))
        o.append(("rs", 2, half))
        for i in range(4 * half, 4 * half + 4):
            o.append(("fin", 2, i))

    names = [m[0] for m in marks]
    ins = {}
    ins.setdefault(marks[0][1] - 40, []).append(("ws", 0))
    for n, (name, at) in enumerate(marks[:-1]):
        ins.setdefault(at, []).append(("ws", n + 1))
    final = []
    stages = []
    for at, step in enumerate(o + [None]):
        for x in ins.get(at, []):
            final.append(x)
        if step:
            final.append(step)
    out = [("wl", 0), ("wl", 1)]
    for step in final:
        out.append(step)
        if step[0] in ("ws", "adaA"):
            stages.append(step)
            out.append(("wl", len(stages) + 1))
    total = len(stages)
    out = [s for s in out if s[0] != "wl" or s[1] < total]
    first = [s for s in out if s[0] == "xl" and s[1] == 0]
    out = first + [s for s in out if s not in first]
    return out, names, stages


def freeing(step):
    k, r = step[0], step[1:]
    if k in ("adaM",):
        return ("adaE", *r), "dve"
    if k == "xT":
        return ("hx", *r), "act"
    if k in ("kvg", "sq", "kT", "gT", "aqT", "apT", "mS", "kN", "yT", "po", "cT", "pq",
             "qrT", "pqT", "pkT", "pv", "mpT", "mO", "mC"):
        return (k + "E", *r), "dve"
    if k == "colsT":
        return ("colsE",), "dve"
    if k in ("lat", "mqk", "mv", "mB", "mo", "z"):
        return (k + "E", *r), "act"
    if k == "asc":
        return ("asm", *r), "act"
    if k == "apv":
        return ("ano", *r), "dve"
    if k == "msc":
        return ("msm", *r[:2]), "act"
    if k == "mpv":
        return ("mno", *r[:2]), "dve"
    return None


def banks_of(step):
    if freeing(step) is None:
        return 0
    if step[0] in ("mS", "mO", "gT"):
        return 2
    if step[0] == "mpv":
        return 1 if step[3] == 0 else 0
    return 1


def trunk(nc, x, ada_w, ada_b, e_in, head_g, sinks, e_out, o_in, uq, ukv, o_out, final_g, columns, gate_b,
          rope, ident_in, small_in, out):
    order, chunk_names, stages = plan()
    nth, seen = {}, {}
    for s in order:
        nth[s] = seen.get(s[0], 0)
        seen[s[0]] = nth[s] + 1
    job, jobs = {}, []
    filled_at = {}
    for s in order:
        if banks_of(s):
            job[s] = len(jobs)
            jobs += [s] * banks_of(s)
    for s in order:
        if s[0] == "mpv":
            job[s] = job["mpv", s[1], s[2], 0]
    for n, s in enumerate(jobs):
        filled_at[s] = n + 1 - 0
    fills = 0
    for s in order:
        if freeing(s) is None:
            continue
        if s[0] == "mpv":
            if s[3] == s[2] // 4:
                fills += 1
                for b in range(s[3] + 1):
                    filled_at["mpv", s[1], s[2], b] = fills
        else:
            fills += banks_of(s)
            filled_at[s] = fills
    chunk_no = {name: n for n, name in enumerate(chunk_names)}
    users = {"kvg": ["kvg"], "uqr": ["pq"]}
    last_job = {}

    def chunk_of(s):
        k = s[0]
        if k == "kvg":
            return "kvg"
        if k in ("sq", "mqk", "mv", "mo", "lat"):
            return s[0], s[1]
        if k == "z":
            return "z", s[1], s[2]
        if k == "po":
            return "out", s[1], s[2]
        if k == "pq":
            return "uqr"
        if k in ("pqT", "pkT", "pv"):
            return "hp", s[1] // 2
        return None

    for s in order:
        if chunk_of(s) is not None:
            last_job[chunk_of(s)] = filled_at[s]
    mat = {"e_in": e_in, "e_out": e_out, "o_in": o_in, "o_out": o_out, "uq": uq, "ukv": ukv}
    stage_no = {s: n for n, s in enumerate(stages)}
    stage_value, per = [], [0, 0]
    for n, s in enumerate(stages):
        count = 2 if s[0] == "adaA" else sum(len(b[3]) for b in CHUNKS[chunk_names[s[1]]])
        per[n % 2] += 16 * count
        stage_value.append(per[n % 2])

    order_at = {(s[0], nth[s]): s for s in order}
    gate_steps = [s for s in order if s[0] == "moE" or s[:2] == ("zE", 0)]
    gate_no = {s: n for n, s in enumerate(gate_steps)}
    qr_dram = nc.dram_tensor("q_rot_scratch", (S, C_HEADS * C_ROPE), F32, kind="Internal").ap()
    x1_dram = nc.dram_tensor("x1_scratch", (S, D), F32, kind="Internal").ap()

    ctx = ExitStack()
    with ctx:
        def sb(name, shape, dt=F32, at=None):
            return (at or ctx).enter_context(nc.sbuf_tensor(name, shape, dt))

        def pair(name, shape, at=None):
            return sb(name + "_hi", shape, F32R, at), sb(name + "_lo", shape, F32R, at)

        bank = [ctx.enter_context(nc.psum_tensor(f"bank{b}", [P, 512], F32)) for b in range(NPSUM)]

        def sem(name):
            return ctx.enter_context(nc.semaphore(name))

        stage = [sb(f"stage{b}", [P, FLAT]) for b in range(2)]
        wsplit = [pair(f"w{b}", [P, FLAT]) for b in range(2)]
        rows = sb("rows", [P, 2, T, 512])
        bias_row = sb("ada_bias_row", [1, 2, CW])
        acc = sb("ada_acc", [P, 2, CW])
        gate_bc = sb("gate_bc", [P, D])
        ident = sb("ident", [P, P])
        small = sb("small_bf16", [P, 640], BF16)
        identb, causal = small[:, 0:128], small[:, 128:256]
        mask_q, mask_k = small[:, 256:384], small[:, 384:640]
        ones = sb("ones", [P, P])
        rope_sb = sb("rope_cs", [P, T, 2 * S_HD])
        cols_in = sb("columns", [P, 45])
        ccol_in = cols_in[:, 0:KD]
        ng = cols_in[:, KD:3 * KD].rearrange("p (l k) -> p l k", l=2)
        cw = cols_in[:, 24:40].rearrange("p (t w) -> p w t", w=4)
        ccol = sb("c_silu", [P, KD])
        amp = sb("amp", [P, 2, KD])
        shift = sb("shift", [P, 2, KD])
        latg = sb("latent_g_col", [P, 6])
        ssq = sb("sum_squares", [P, 2 * T])
        rstd = sb("rstd", [P, 2 * T])
        nt = sb("newton", [P, 3, 32])
        tmp = sb("act_tmp", [P, 512])
        dtmp = sb("dve_tmp", [P, 512])
        even = ExitStack()
        hT = pair("hT", [P, KD, S], even)
        negM = sb("m_neg_max_row", [M_HEADS, S], F32, even)
        hg = sb("head_g_bc", [P, M_HEADS * M_DV], F32, even)
        gate_b_col = sb("gate_bias_col", [M_HEADS, 2], F32, even)
        sink_bc = sb("sink_bc", [P, S_QH], F32, even)
        ifn = sb("gate_rows", [P, T, 2 * M_HEADS], F32, even)
        gcol = sb("m_g_col", [P, T, M_HEADS], F32, even)
        mcols = sb("m_cols", [P, 160], F32, even)
        margs = sb("m_exponents", [P, 4, T, M_HEADS], F32, even)
        mden = sb("m_den", [P, T, M_HEADS], F32, even)
        hss = sb("m_sum_squares", [P, T, M_HEADS], F32, even)
        msc_t = sb("m_scale", [P, T, M_HEADS], F32, even)
        norm_mem = ExitStack()
        xhat = sb("xhat", [P, T, D], F32, norm_mem)
        norm_mem.close()
        win = ExitStack()
        vs = pair("s_v", [P, T, P], win)
        ksT = pair("s_kT", [P, S], win)
        qsT = pair("s_qT", [P, S_G, P], win)
        sp = sb("s_probs", [P, 2, 2, 256], F32, win)
        spT = [pair(f"s_pT{b}", [P, 2, 2, P], win) for b in range(2)]
        sst = sb("s_stats", [P, 4, 12], F32, win)
        win.close()
        mem = ExitStack()
        raw = sb("m_raw", [P, S + 3], F32, mem)
        cacc = sb("m_conv", [P, S], F32, mem)
        qmT = pair("m_qT", [P, S], mem)
        kmT = pair("m_kT", [P, S], mem)
        vm = [pair(f"m_v{b}", [P, 2, VW], mem) for b in range(2)]
        Wt = sb("m_W", [P, 2, 2, P], F32, mem)
        sw = pair("m_S", [P, 2, P], mem)
        kw = pair("m_kw", [P, P], mem)
        htile = sb("m_h", [P, VW], F32, mem)
        Cst = sb("m_C", [P, VW], F32, mem)
        Csp = pair("m_Cs", [P, VW], mem)
        mem.close()
        even.close()
        fin_mem = ExitStack()
        sb("place_of_hT_a", [P, 2, KD, S], F32, fin_mem)
        final_bc = sb("final_g_bc", [P, D], F32, fin_mem)
        fin_mem.close()
        lat = ExitStack()
        sb("place_of_hT_b", [P, 2, KD, S], F32, lat)
        craw = sb("c_rows", [P, T, CRW], F32, lat)
        lat.close()
        late = ExitStack()
        cT = pair("c_T", [P, 6, S], late)
        qrT = pair("c_qrT", [P, S], late)
        qmain = pair("c_qT", [P, S], late)
        kT = pair("c_kT", [P, S], late)
        vT = pair("c_v", [P, T, P], late)
        qrow = sb("c_q_rot_rows", [P, T, P], F32, late)
        cp = sb("c_probs", [P, 2, S], F32, late)
        cpT = [pair(f"c_pT{b}", [P, 4, P], late) for b in range(3)]
        cst = sb("c_stats", [P, 4, 8], F32, late)
        late.close()

        filled = sem("psum_filled")
        vector_done = {}
        scalar_done = {}
        for s_ in order:
            k = s_[0]
            if k in DVE_KINDS and k not in vector_done:
                vector_done[k] = sem("vector_done_" + k)
            if k in ACT_KINDS and k not in scalar_done:
                scalar_done[k] = sem("scalar_done_" + k)
        split_done = sem("weight_chunks_split")
        v_split = sem("mlstm_v_split")
        dve_step = sem("vector_step")
        act_step = sem("scalar_step")
        const_in = sem("constants_in")
        even_in = sem("even_constants_in")
        final_in = sem("final_g_in")
        stage_in = [sem(f"stage{b}_in") for b in range(2)]
        x_in = [sem(f"x{i}_in") for i in range(T)]
        x_out = [sem(f"x1_{i}_out") for i in range(T)]
        qrot_out = [sem(f"q_rot_out{b}") for b in range(2)]
        qrot_in = sem("q_rot_in")
        y_out = sem("y_out")

        hx_tmp = [tmp, dtmp]
        tmp2 = tmp

        def bank_of(*step, m=0):
            return bank[(job[step] + m) % NPSUM]

        def grow(n):
            return rows[0:M_HEADS, 0, 2 * n:2 * n + 2, :].rearrange("p t d -> p (t d)")

        kn = rows[:, 0, 6:8, :].rearrange("p t d -> p (t d)").rearrange("p (t d) -> p t d", d=P)

        def split_dst(step):
            k, r = step[0], step[1:]
            cols = lambda half: slice(512 * half, 512 * half + 512)
            if k == "kTE":
                return [a[:, cols(r[0])] for a in ksT]
            if k == "aqTE":
                return [a[:, :, :].rearrange("p a q -> p (a q)") for a in qsT]
            if k == "apTE":
                return [a[:, :, 0:2, :] if r[0] else a[:, :, 1:2, :] for a in spT[nth[step] % 2]]
            if k == "yTE":
                return [a[:, r[1], cols(r[2])] for a in hT]
            if k == "cTE":
                return [a[:, r[0], cols(r[1])] for a in cT]
            if k == "qrTE":
                return [a[:, cols(r[1])] for a in qrT]
            if k == "pqTE":
                return [a[:, cols(r[1])] for a in qmain]
            if k == "pkTE":
                return [a[:, cols(r[1])] for a in kT]
            if k == "pvE":
                return [a[:, 4 * r[1]:4 * r[1] + 4, :].rearrange("p t d -> p (t d)") for a in vT]
            n = min(4, r[1] + 1 - 4 * r[2])
            return [a[:, 0:n, :].rearrange("p t d -> p (t d)") for a in cpT[nth[step] % 3]]

        def shaped(b, step):
            if step[0] == "apTE":
                v = b[:, :].rearrange("p (j k q) -> p j k q", j=2, k=2)
                return v if step[1] else v[:, :, 1:2, :]
            if step[0] == "mpTE":
                return b[:, 0:P * min(4, step[2] + 1 - 4 * step[3])]
            return b[:, :]

        CONSTS = 16 * 4
        EVEN_CONSTS = 16 * 3
        block = ctx.enter_context(nc.Block())

        @block.sync
        def _(sp_eng):
            def const(dst, src, s_):
                sp_eng.dma_start(dst, src).then_inc(s_, 16)

            begun = False
            for step in order:
                k = step[0]
                if k == "xl":
                    l, i = step[1:]
                    if l == 2:
                        sp_eng.wait_ge(filled, filled_at["yT", 0, KD - 1, i // 4])
                    if l == 3:
                        sp_eng.wait_ge(filled, filled_at["yT", 1, KD - 1, i // 4])
                        sp_eng.wait_ge(x_out[i], 16)
                    src = x1_dram if l == 3 else x
                    sp_eng.dma_start(rows[:, :, i, :], src[i * P:(i + 1) * P, :].rearrange("p (a d) -> p a d", a=2))\
                        .then_inc(x_in[i], 16)
                    if l == 0 and i == 3 and not begun:
                        begun = True
                        const(cols_in[:, :], columns, const_in)
                        const(ident[:, :], ident_in, const_in)
                        const(rope_sb[:, :, :], rope.rearrange("(t p) c -> p t c", p=P), const_in)
                        const(gate_bc[:, 0:640], small_in, const_in)
                        const(hg[:, :], head_g.rearrange("a d -> (a d)").partition_broadcast(P), even_in)
                        const(sink_bc[:, :], sinks.rearrange("a d -> (a d)").partition_broadcast(P), even_in)
                        const(gate_b_col[:, :], gate_b, even_in)
                elif k == "wl":
                    n = step[1]
                    what = stages[n]
                    if n >= 2:
                        before = stages[n - 2]
                        if before[0] == "ws":
                            sp_eng.wait_ge(split_done, before[1] + 1)
                        else:
                            sp_eng.wait_ge(vector_done[before[0]], nth[before] + 1)
                    buf = stage[n % 2]
                    if what[0] == "adaA":
                        _, l, cc = what
                        sp_eng.dma_start(buf[:, 0:KD * CW].rearrange("p (k w) -> p k w", k=KD),
                                         ada_w[l].rearrange("(k p) n -> p k n", p=P)[:, :, CW * cc:CW * (cc + 1)])\
                            .then_inc(stage_in[n % 2], 16)
                        sp_eng.dma_start(bias_row[:, n % 2, :], ada_b[l:l + 1, CW * cc:CW * (cc + 1)])\
                            .then_inc(stage_in[n % 2], 16)
                    else:
                        for off, kt, width, pieces in CHUNKS[chunk_names[what[1]]]:
                            view = buf[:, off:off + kt * width].rearrange("p (k w) -> p k w", k=kt)
                            for name, col, w, to in pieces:
                                src = mat[name][0].rearrange("(k p) n -> p k n", p=P)
                                sp_eng.dma_start(view[:, :, to:to + w], src[:, :, col:col + w])\
                                    .then_inc(stage_in[n % 2], 16)
                elif k == "xs":
                    i = step[1]
                    sp_eng.wait_ge(vector_done["poE"], nth["poE", 0, 3, i] + 1)
                    sp_eng.dma_start(x1_dram[i * P:(i + 1) * P, :].rearrange("p (a d) -> p a d", a=2),
                                     rows[:, :, i, :]).then_inc(x_out[i], 16)
                elif k == "qs":
                    i = step[1]
                    sp_eng.wait_ge(vector_done["pqE"], nth["pqE", i] + 1)
                    sp_eng.dma_start(qr_dram[i * P:(i + 1) * P, :], cp[:, i % 2, 0:512]).then_inc(qrot_out[i % 2], 16)
                elif k == "ql":
                    a = step[1]
                    if a == 0:
                        for b in range(2):
                            sp_eng.wait_ge(qrot_out[b], 16 * T // 2)
                    else:
                        sp_eng.wait_ge(filled, filled_at["qrT", a - 1, 1])
                    sp_eng.dma_start(qrow[:, :, :], qr_dram.rearrange("(t p) c -> p t c", p=P)[:, :, P * a:P * (a + 1)])\
                        .then_inc(qrot_in, 16)
                elif k == "fin":
                    i = step[2]
                    if i == 0:
                        pass
                    sp_eng.wait_ge(vector_done[k], nth[step] + 1)
                    sp_eng.dma_start(out[0, i * P:(i + 1) * P, :], xhat[:, i, :]).then_inc(y_out, 16)
                elif k == "fg":
                    sp_eng.wait_ge(filled, filled_at["yT", 1, 0, 0])
                    sp_eng.dma_start(final_bc[:, :], final_g.partition_broadcast(P)).then_inc(final_in, 16)
            sp_eng.wait_ge(y_out, 16 * T)

        @block.gpsimd
        def _(pool):
            for step in order:
                if step[0] == "ws":
                    n = step[1]
                    size = max(b[0] + b[1] * b[2] for b in CHUNKS[chunk_names[n]])
                    pool.wait_ge(scalar_done[step[0]], nth[step] + 1)
                    nc.gpsimd.tensor_tensor(wsplit[n % 2][1][:, 0:size], stage[stage_no[step] % 2][:, 0:size],
                                            wsplit[n % 2][0][:, 0:size].bitcast(F32), ALU.subtract)\
                        .then_inc(split_done, 1)
                elif step[0] == "vsp":
                    _, p, i = step
                    pool.wait_ge(scalar_done[step[0]], nth[step] + 1)
                    nc.gpsimd.tensor_tensor(vm[i % 2][1][:, :, 0:M_DV],
                                            rows[:, 0, i, CW * p:CW * (p + 1)].rearrange("p (h d) -> p h d", h=2),
                                            vm[i % 2][0][:, :, 0:M_DV].bitcast(F32), ALU.subtract)\
                        .then_inc(v_split, 1)

        @block.tensor
        def _(pe):
            def start(step, m=0):
                n = job[step] + m
                if n >= NPSUM:
                    free, who = freeing(jobs[n - NPSUM])
                    if who == "dve":
                        pe.wait_ge(vector_done[free[0]], nth[free] + 1)
                    else:
                        pe.wait_ge(scalar_done[free[0]], nth[free] + 1)
                return bank[n % NPSUM]

            def mm3(o, a, b, at, bt, first, last, **kw):
                pe.matmul(o, a[0][at], b[0][bt], start=first, stop=False, **kw)
                pe.matmul(o, a[0][at], b[1][bt], start=False, stop=False, **kw)
                return pe.matmul(o, a[1][at], b[0][bt], start=False, stop=last, **kw)

            def weights(name):
                pe.wait_ge(split_done, chunk_no[name] + 1)
                return wsplit[chunk_no[name] % 2]

            def project(step, name, i, width):
                o = start(step)
                w = weights(name)
                for k in range(KD):
                    last = mm3(o[:, 0:width], hT, w, (slice(None), k, slice(i * P, (i + 1) * P)),
                               (slice(None), slice(k * width, (k + 1) * width)), k == 0, k == KD - 1)
                last.then_inc(filled, 1)

            def turn4(step, srcs, n=4):
                o = start(step)
                for j, src in enumerate(srcs):
                    if src is not None:
                        last = pe.transpose(o[:, j * P:(j + 1) * P], src, ident[:, :])
                last.then_inc(filled, 1)

            pe.wait_ge(const_in, CONSTS)
            pe.wait_ge(vector_done["ones"], nth["ones",] + 1)
            for step in order:
                k, r = step[0], step[1:]
                if k == "adaM":
                    l, cc = r
                    o = start(step)
                    pe.wait_ge(vector_done["adaA"], nth["adaA", l, cc] + 1)
                    a = acc[:, nth[step] % 2, :]
                    if cc < 8:
                        for j in range(2):
                            last = pe.matmul(o[:, j:j + 1], a[:, j * P:(j + 1) * P], ones[:, 0:1], start=True, stop=True)
                    else:
                        last = pe.matmul(o[:, 0:CW], ones[:, :], a, start=True, stop=True)
                    last.then_inc(filled, 1)
                elif k == "xT":
                    l, kk, half = r
                    pe.wait_ge(vector_done["xh"], nth["xh", l, 4 * half + 3] + 1)
                    turn4(step, [xhat[:, i, kk * P:(kk + 1) * P] for i in range(4 * half, 4 * half + 4)])
                elif k == "kvg":
                    pe.wait_ge(vector_done["hx"], nth["hx", 0, KD - 1, r[0] // 4] + 1)
                    project(step, "kvg", r[0], 264)
                elif k == "sq":
                    project(step, ("sq", r[0]), r[1], CW)
                elif k == "gT":
                    half = r[0]
                    pe.wait_ge(scalar_done["kvgE"], nth["kvgE", 4 * half + 3] + 1)
                    for m in range(2):
                        o = start(step, m)
                        for ii in range(4):
                            last = pe.transpose(o[0:M_HEADS, ii * P:(ii + 1) * P],
                                                ifn[:, 4 * half + ii, M_HEADS * m:M_HEADS * (m + 1)], ident[:, :])
                        last.then_inc(filled, 1)
                elif k == "kT":
                    pe.wait_ge(vector_done["kvgE"], nth["kvgE", 4 * r[0] + 3] + 1)
                    turn4(step, [kn[:, i, :] for i in range(4 * r[0], 4 * r[0] + 4)])
                elif k == "aqT":
                    pe.wait_ge(vector_done["sqE"], nth["sqE", 1, r[0]] + 1)
                    turn4(step, [rows[:, 1, r[0], j * P:(j + 1) * P] for j in range(4)])
                elif k == "asc":
                    i, g, ap = r
                    pe.wait_ge(vector_done["aqTE"], nth["aqTE", i] + 1)
                    pe.wait_ge(vector_done["kTE"], nth["kTE", 1 if i > 3 else 0] + 1)
                    o = start(step)
                    part = slice(64 * g, 64 * g + 64)
                    lo_key, at = ((i - 1) * P, 0) if i else (0, P)
                    for j in range(2):
                        dst = o[:, 256 * j + at:256 * j + 256]
                        mm3(dst, qsT, ksT, (part, 2 * ap + j, slice(None)), (part, slice(lo_key, (i + 1) * P)), True, False)
                        last = pe.matmul(dst, mask_q[part, :], mask_k[part, at:256], start=False, stop=True)
                    last.then_inc(filled, 1)
                elif k == "apT":
                    i, g, ap = r
                    pe.wait_ge(scalar_done["asm"], nth["asm", i, g, ap] + 1)
                    u = nth["asm", i, g, ap] % 2
                    turn4(step, [sp[:, u, j // 2, (j % 2) * P:(j % 2 + 1) * P] if i or j % 2 else None for j in range(4)])
                elif k == "apv":
                    i, g, ap = r
                    pe.wait_ge(vector_done["apTE"], nth["apTE", i, g, ap] + 1)
                    pe.wait_ge(vector_done["kvgE"], nth["kvgE", i] + 1)
                    o = start(step)
                    u = nth["apTE", i, g, ap] % 2
                    kts = (0, 1) if i else (1,)
                    for j in range(2):
                        for kt in kts:
                            last = mm3(o[:, 64 * j:64 * j + 64], spT[u], vs, (slice(None), j, kt, slice(None)),
                                       (slice(None), i - 1 + kt, slice(64 * g, 64 * g + 64)), kt == kts[0], kt == 1)
                    last.then_inc(filled, 1)
                elif k == "colsT":
                    pe.wait_ge(vector_done["rows"], nth["rows",] + 1)
                    o = start(step)
                    for q, src in enumerate((grow(0), negM[:, :], grow(2))):
                        for i in range(T):
                            pe.transpose(o[:, 32 * q + 4 * i:32 * q + 4 * i + 4], src[:, i * P:(i + 1) * P],
                                         ident[0:M_HEADS, 0:M_HEADS])
                    for q, src in enumerate((grow(2), negM[:, :])):
                        for h in range(M_HEADS):
                            at = 96 + 32 * q + 8 * h
                            last = pe.matmul(o[:, at:at + T], ident[0:M_HEADS, h:h + 1].broadcast_to([M_HEADS, P]),
                                             src.rearrange("h (t s) -> h t s", s=P)[:, :, P - 1], start=True, stop=True)
                    last.then_inc(filled, 1)
                elif k == "mqk":
                    p, which, half = r
                    o = start(step)
                    w = weights(("mqk", p))
                    for kk in range(KD):
                        last = mm3(o[:, :], w, hT, (slice(None), slice(kk * CW + P * which, kk * CW + P * which + P)),
                                   (slice(None), kk, slice(512 * half, 512 * half + 512)), kk == 0, kk == KD - 1)
                    last.then_inc(filled, 1)
                elif k == "mv":
                    project(step, ("mv", r[0]), r[1], CW)
                elif k == "mB":
                    p, i = r
                    o = start(step)
                    if p == 0 and i == 0:
                        pe.wait_ge(vector_done["rows"], nth["rows",] + 1)
                    for j in range(2):
                        h = 2 * p + j
                        dst = o[:, j * P:(j + 1) * P]
                        pe.matmul(dst, ident[0:M_HEADS, h:h + 1].broadcast_to([M_HEADS, P]),
                                  negM[:, i * P:(i + 1) * P], start=True, stop=False)
                        last = pe.matmul(dst, identb, causal, start=False, stop=True)
                    last.then_inc(filled, 1)
                elif k == "mS":
                    p, i = r
                    pe.wait_ge(vector_done["conv"], nth["conv", p, 1] + 1)
                    pe.wait_ge(vector_done["qksp"], nth["qksp", p, 1] + 1)
                    for j in range(2):
                        o = start(step, j)
                        at = (slice(64 * j, 64 * j + 64), slice(i * P, (i + 1) * P))
                        mm3(o[:, 0:P], kmT, qmT, at, at, True, True).then_inc(filled, 1)
                elif k == "kN":
                    p, i = r
                    turn4(step, [cacc[:, i * P:(i + 1) * P]])
                elif k == "mO":
                    p, i = r
                    pe.wait_ge(vector_done["mSE"], nth["mSE", p, i] + 1)
                    pe.wait_ge(v_split, T * p + i + 1)
                    for j in range(2):
                        o = start(step, j)
                        last = mm3(o[:, 0:VW], sw, vm[i % 2], (slice(None), j, slice(None)), (slice(None), j, slice(None)),
                                   True, True)
                        if i:
                            pe.wait_ge(vector_done["mCE"], nth["mCE", p, i - 1] + 1)
                            part = slice(64 * j, 64 * j + 64)
                            last = mm3(o[:, 256:256 + VW], qmT, Csp, (part, slice(i * P, (i + 1) * P)),
                                       (part, slice(None)), True, True)
                        last.then_inc(filled, 1)
                elif k == "mC":
                    p, i = r
                    pe.wait_ge(vector_done["kNE"], nth["kNE", p, i] + 1)
                    o = start(step)
                    for j in range(2):
                        last = mm3(o[:, 256 * j:256 * j + VW], kw, vm[i % 2], (slice(None), slice(None)),
                                   (slice(None), j, slice(None)), True, True)
                    last.then_inc(filled, 1)
                elif k == "mo":
                    project(step, ("mo", r[0]), r[1], CW)
                elif k == "z":
                    project(step, ("z", r[0], r[1]), r[2], CW)
                elif k == "yT":
                    l, kk, half = r
                    if l == 0:
                        pe.wait_ge(vector_done["zE"], nth["zE", 0, kk // 2, 4 * half + 3] + 1)
                    else:
                        pe.wait_ge(vector_done["mno"], nth["mno", C_HEADS - 1, T - 1] + 1)
                    turn4(step, [rows[:, kk // 4, i, (kk % 4) * P:(kk % 4 + 1) * P] for i in range(4 * half, 4 * half + 4)])
                elif k == "po":
                    l, oc, i = r
                    pe.wait_ge(vector_done["yTE"], nth["yTE", l, KD - 1, i // 4] + 1)
                    project(step, ("out", l, oc), i, CW)
                elif k == "lat":
                    cc, i = r
                    pe.wait_ge(vector_done["hx"], nth["hx", 1, KD - 1, i // 4] + 1)
                    project(step, ("lat", cc), i, LAT_W[cc])
                elif k == "cT":
                    kk, half = r
                    pe.wait_ge(vector_done["lsc"], nth["lsc", 4 * half + 3] + 1)
                    turn4(step, [craw[:, i, kk * P:(kk + 1) * P] for i in range(4 * half, 4 * half + 4)])
                elif k == "pq":
                    i = r[0]
                    pe.wait_ge(vector_done["cTE"], nth["cTE", 5, 1] + 1)
                    o = start(step)
                    w = weights("uqr")
                    for kk in range(KQ):
                        last = mm3(o[:, :], cT, w, (slice(None), kk, slice(i * P, (i + 1) * P)),
                                   (slice(None), slice(kk * 512, (kk + 1) * 512)), kk == 0, kk == KQ - 1)
                    last.then_inc(filled, 1)
                elif k == "qrT":
                    a, half = r
                    pe.wait_ge(qrot_in, 16 * (a + 1))
                    turn4(step, [qrow[:, i, :] for i in range(4 * half, 4 * half + 4)])
                elif k in ("pqT", "pkT"):
                    h, half = r
                    o = start(step)
                    w = weights(("hp", h // 2))
                    j, kts = h % 2, KQ if k == "pqT" else KKV
                    for kk in range(kts):
                        at = kk * 256 + P * j if k == "pqT" else 768 + kk * 512 + 256 * j
                        row = kk if k == "pqT" else KQ + kk
                        last = mm3(o[:, :], w, cT, (slice(None), slice(at, at + P)),
                                   (slice(None), row, slice(512 * half, 512 * half + 512)), kk == 0, kk == kts - 1)
                    last.then_inc(filled, 1)
                elif k == "pv":
                    h, half = r
                    o = start(step)
                    w = weights(("hp", h // 2))
                    for ii in range(4):
                        i = 4 * half + ii
                        for kk in range(KKV):
                            at = 768 + kk * 512 + 256 * (h % 2) + P
                            last = mm3(o[:, ii * P:(ii + 1) * P], cT, w, (slice(None), KQ + kk, slice(i * P, (i + 1) * P)),
                                       (slice(None), slice(at, at + P)), kk == 0, kk == KKV - 1)
                    last.then_inc(filled, 1)
                elif k == "msc":
                    h, i, b = r
                    pe.wait_ge(vector_done["pqTE"], nth["pqTE", h, i // 4] + 1)
                    pe.wait_ge(vector_done["pkTE"], nth["pkTE", h, i // 4] + 1)
                    pe.wait_ge(vector_done["qrTE"], nth["qrTE", h // 2, i // 4] + 1)
                    o = start(step)
                    nk = min(512, P * (i + 1) - 512 * b)
                    part = slice(64 * (h % 2), 64 * (h % 2) + 64)
                    keys, tile = slice(512 * b, 512 * b + nk), slice(i * P, (i + 1) * P)
                    mm3(o[:, 0:nk], qmain, kT, (slice(None), tile), (slice(None), keys), True, False)
                    diagonal = 512 * b + nk == P * (i + 1)
                    if diagonal:
                        pe.matmul(o[:, nk - P:nk], mask_q[part, :], mask_k[part, P:256], start=False, stop=False,
                                  skip_group_check=True)
                    last = mm3(o[:, 0:nk], qrT, cT, (part, tile), (part, 5, keys), False, True)
                    last.then_inc(filled, 1)
                elif k == "mpT":
                    h, i, b = r
                    pe.wait_ge(scalar_done["msm"], nth["msm", h, i] + 1)
                    u = nth["msm", h, i] % 2
                    n = min(4, i + 1 - 4 * b)
                    turn4(step, [cp[:, u, (4 * b + j) * P:(4 * b + j + 1) * P] for j in range(n)])
                elif k == "mpv":
                    h, i, b = r
                    pe.wait_ge(vector_done["mpTE"], nth["mpTE", h, i, b] + 1)
                    pe.wait_ge(vector_done["pvE"], nth["pvE", h, i // 4] + 1)
                    o = start(step) if b == 0 else bank[job[step] % NPSUM]
                    src = cpT[nth["mpTE", h, i, b] % 3]
                    for j in range(min(4, i + 1 - 4 * b)):
                        kt = 4 * b + j
                        last = mm3(o[:, 0:P], src, vT, (slice(None), j, slice(None)), (slice(None), kt, slice(None)),
                                   kt == 0, kt == i)
                    if b == i // 4:
                        last.then_inc(filled, 1)

        @block.scalar
        def _(act):
            steps_done = [0]

            def again(ins):
                steps_done[0] += 1
                ins.then_inc(act_step, 1)
                act.wait_ge(act_step, steps_done[0])

            act.wait_ge(const_in, CONSTS)
            before = None
            for step in order:
                k, r = step[0], step[1:]
                if k not in ACT_KINDS:
                    continue
                if before:
                    act.wait_ge(scalar_done[before[0]], nth[before] + 1)
                before = step
                done = scalar_done[k]
                if k == "csilu":
                    nc.scalar.activation(ccol[:, :], ccol_in, ACT.Silu).then_inc(done, 1)
                elif k == "ws":
                    n = r[0]
                    s_no = stage_no[step]
                    size = max(b[0] + b[1] * b[2] for b in CHUNKS[chunk_names[n]])
                    act.wait_ge(stage_in[s_no % 2], stage_value[s_no])
                    if n >= 2:
                        act.wait_ge(filled, last_job[chunk_names[n - 2]])
                    nc.scalar.activation(wsplit[n % 2][0][:, 0:size], stage[s_no % 2][:, 0:size], ACT.Copy)\
                        .then_inc(done, 1)
                elif k == "xsq":
                    l, i = r
                    if l == 0:
                        act.wait_ge(x_in[i], 16)
                    else:
                        act.wait_ge(vector_done["poE"], nth["poE", l - 1, 3, i] + 1)
                    nc.scalar.activation(xhat[:, i, :].rearrange("p (a d) -> p a d", a=2), rows[:, :, i, :], ACT.Square,
                                         accum_out=ssq[:, i:i + 1]).then_inc(done, 1)
                elif k == "hx":
                    l, kk, half = r
                    act.wait_ge(filled, filled_at["xT", l, kk, half])
                    if kk == 0 and half == 0:
                        act.wait_ge(vector_done["adaE"], nth["adaE", l, 7] + 1)
                    if nth[step] >= 2:
                        act.wait_ge(vector_done["hx"], nth[step] - 1)
                    nc.scalar.activation(hx_tmp[nth[step] % 2][:, :],
                                         bank_of("xT", *r)[:, :], ACT.Identity,
                                         bias=shift[:, l, kk:kk + 1], scale=amp[:, l, kk:kk + 1]).then_inc(done, 1)
                elif k == "kvgE":
                    i = r[0]
                    act.wait_ge(filled, filled_at["kvg", i])
                    b = bank_of("kvg", i)
                    nc.scalar.activation(vs[0][:, i, :], b[:, 128:256], ACT.Copy)
                    nc.scalar.activation(ifn[:, i, :], b[:, 256:264], ACT.Copy).then_inc(done, 1)
                elif k in ("kTE", "aqTE", "apTE", "yTE", "qrTE", "pqTE", "pkTE", "pvE", "mpTE", "cTE"):
                    src = (k[:-1], *r)
                    act.wait_ge(filled, filled_at[src])
                    b = bank_of(*src)
                    hi = split_dst(step)[0]
                    if k == "apTE" and nth[step] >= 2:
                        act.wait_ge(filled, filled_at["apv", *order_at[k, nth[step] - 2][1:]])
                    if k == "mpTE" and nth[step] >= 3:
                        act.wait_ge(filled, filled_at["mpv", *order_at[k, nth[step] - 3][1:]])
                    scale = latg[:, r[0]:r[0] + 1] if k == "cTE" else 1.0
                    if k == "cTE":
                        act.wait_ge(vector_done["ones"], nth["ones",] + 1)
                    nc.scalar.activation(hi, shaped(b, step), ACT.Copy, scale=scale).then_inc(done, 1)
                elif k == "rowsB":
                    act.wait_ge(vector_done["rowsA"], nth["rowsA",] + 1)
                    again(nc.scalar.activation(grow(2), grow(2), ACT.Exp))
                    nc.scalar.activation(grow(2), grow(2), ACT.Ln, bias=1.0).then_inc(done, 1)
                elif k == "asm":
                    i, g, ap = r
                    act.wait_ge(filled, filled_at["asc", *r])
                    act.wait_ge(vector_done[k], nth[step] + 1)
                    u = nth[step] % 2
                    st = sst[:, nth[step] % 4, :]
                    if nth[step] >= 2:
                        act.wait_ge(filled, filled_at["apT", *order_at["asm", nth[step] - 2][1:]])
                    b = bank_of("asc", *r)
                    at = 0 if i else P
                    nc.scalar.activation(st[:, 4:6], st[:, 4:6], ACT.Exp)
                    for j in range(2):
                        last = nc.scalar.activation(sp[:, u, j, at:256], b[:, 256 * j + at:256 * j + 256], ACT.Exp,
                                                    bias=st[:, 2 + j:3 + j], scale=S_SCALE,
                                                    accum_out=st[:, 6 + j:7 + j])
                    last.then_inc(done, 1)
                elif k == "cols":
                    act.wait_ge(vector_done["colsE"], nth["colsE",] + 1)
                    nc.scalar.activation(margs[:, :, :, :], margs[:, :, :, :], ACT.Exp).then_inc(done, 1)
                elif k == "mqkE":
                    p, which, half = r
                    act.wait_ge(filled, filled_at["mqk", *r])
                    if which or p:
                        act.wait_ge(vector_done["conv"], nth["conv", p if which else p - 1, 0 if which else 1] + 1)
                    else:
                        act.wait_ge(vector_done["cols"], nth["cols",] + 1)
                    nc.scalar.activation(raw[:, 3 + 512 * half:3 + 512 * half + 512], bank_of("mqk", *r)[:, :],
                                         ACT.Copy).then_inc(done, 1)
                elif k == "silu":
                    p, which = r
                    act.wait_ge(vector_done["conv"], nth["conv", p, which] + 1)
                    again(nc.scalar.activation(cacc[:, :], cacc[:, :], ACT.Silu))
                    nc.scalar.activation((kmT if which else qmT)[0][:, :], cacc[:, :], ACT.Copy,
                                         scale=M_SCALE if which else 1.0).then_inc(done, 1)
                elif k == "mvE":
                    p, i = r
                    act.wait_ge(filled, filled_at["mv", p, i])
                    nc.scalar.activation(rows[:, 0, i, CW * p:CW * (p + 1)], bank_of("mv", p, i)[:, 0:CW], ACT.Copy)\
                        .then_inc(done, 1)
                elif k == "vsp":
                    p, i = r
                    if p or i >= 2:
                        b = ("vsp", p, i - 2) if i >= 2 else ("vsp", p - 1, i + T - 2)
                        act.wait_ge(filled, filled_at["mC" if b[2] < T - 1 else "mO", *b[1:]])
                    else:
                        act.wait_ge(vector_done["cols"], nth["cols",] + 1)
                    act.wait_ge(scalar_done["mvE"], nth["mvE", p, i] + 1)
                    nc.scalar.activation(vm[i % 2][0][:, :, 0:M_DV],
                                         rows[:, 0, i, CW * p:CW * (p + 1)].rearrange("p (h d) -> p h d", h=2),
                                         ACT.Copy).then_inc(done, 1)
                elif k == "mBE":
                    p, i = r
                    act.wait_ge(filled, filled_at["mB", p, i])
                    if nth[step] >= 2:
                        act.wait_ge(vector_done["mSE"], nth[step] - 1)
                    for j in range(2):
                        last = nc.scalar.activation(Wt[:, nth[step] % 2, j, :], bank_of("mB", p, i)[:, j * P:(j + 1) * P],
                                                    ACT.Exp, bias=gcol[:, i, 2 * p + j:2 * p + j + 1])
                    last.then_inc(done, 1)
                elif k == "hsq":
                    p, i = r
                    act.wait_ge(vector_done["mOE"], nth["mOE", p, i] + 1)
                    for j in range(2):
                        h = 2 * p + j
                        last = nc.scalar.activation(tmp[:, M_DV * j:M_DV * (j + 1)], rows[:, 0, i, M_DV * h:M_DV * (h + 1)], ACT.Square,
                                                    accum_out=hss[:, i, h:h + 1])
                    last.then_inc(done, 1)
                elif k in ("moE", "zE"):
                    src = (k[:-1], *r)
                    act.wait_ge(filled, filled_at[src])
                    b = bank_of(*src)
                    i = r[-1]
                    if k == "zE" and r[0] == 1:
                        zc = r[1]
                        act.wait_ge(x_out[i], 16)
                        act.wait_ge(vector_done["xh"], nth["xh", 1, i] + 1)
                        nc.scalar.activation(rows[:, zc // 2, i, CW * (zc % 2):CW * (zc % 2 + 1)], b[:, 0:CW], ACT.Silu)\
                            .then_inc(done, 1)
                    else:
                        par = gate_no[step] % 2
                        if gate_no[step] >= 2:
                            act.wait_ge(vector_done[gate_steps[gate_no[step] - 2][0]], nth[gate_steps[gate_no[step] - 2]] + 1)
                        nc.scalar.activation(tmp[:, CW * par:CW * (par + 1)], b[:, 0:CW],
                                             ACT.Tanh if k == "moE" else ACT.Silu,
                                             scale=0.5 if k == "moE" else 1.0).then_inc(done, 1)
                elif k == "latE":
                    cc, i = r
                    act.wait_ge(filled, filled_at["lat", cc, i])
                    nc.scalar.activation(craw[:, i, CW * cc:CW * cc + LAT_W[cc]], bank_of("lat", cc, i)[:, 0:LAT_W[cc]],
                                         ACT.Copy).then_inc(done, 1)
                elif k == "lsq":
                    i = r[0]
                    act.wait_ge(scalar_done["latE"], nth["latE", 2, i] + 1)
                    again(nc.scalar.activation(tmp[:, 0:C_QL], craw[:, i, 0:C_QL], ACT.Square, accum_out=ssq[:, i:i + 1]))
                    nc.scalar.activation(tmp[:, 0:C_KVL], craw[:, i, C_QL:C_QL + C_KVL], ACT.Square,
                                         accum_out=ssq[:, T + i:T + i + 1]).then_inc(done, 1)
                elif k == "msm":
                    h, i = r
                    act.wait_ge(vector_done[k], nth[step] + 1)
                    u = nth[step] % 2
                    st = cst[:, nth[step] % 4, :]
                    if nth[step] >= 2:
                        b = order_at["msm", nth[step] - 2]
                        act.wait_ge(filled, filled_at["mpT", b[1], b[2], b[2] // 4])
                    for b in range(i // 4 + 1):
                        nk = min(512, P * (i + 1) - 512 * b)
                        last = nc.scalar.activation(cp[:, u, 512 * b:512 * b + nk], bank_of("msc", h, i, b)[:, 0:nk],
                                                    ACT.Exp, bias=st[:, 2:3], scale=C_SCALE,
                                                    accum_out=st[:, 3 + b:4 + b])
                    last.then_inc(done, 1)

        @block.vector
        def _(dve):
            steps_done = [0]

            def again(ins):
                steps_done[0] += 1
                ins.then_inc(dve_step, 1)
                dve.wait_ge(dve_step, steps_done[0])

            V = nc.vector

            def rotate(dst, src, i, n, done=None):
                cos = rope_sb[:, i:i + 1, 0:64].broadcast_to([P, n, 64])
                a = dtmp[:, 0:64 * n].rearrange("p (n d) -> p n d", d=64)
                b = tmp2[:, 0:64 * n].rearrange("p (n d) -> p n d", d=64)
                V.tensor_tensor(a, src, cos, ALU.mult)
                for m in range(2):
                    sin = rope_sb[:, i:i + 1, 64 + 32 * m:96 + 32 * m].broadcast_to([P, n, 32])
                    last = V.tensor_tensor(b[:, :, 32 * m:32 * m + 32], src[:, :, 32 * (1 - m):32 * (1 - m) + 32], sin, ALU.mult)
                again(last)
                ins = V.tensor_tensor(dst, a, b, ALU.add)
                if done:
                    ins.then_inc(done, 1)
                return ins

            def inverse_root(dst, v, n, done):
                y, a = nt[:, 1, 0:n], nt[:, 2, 0:n]
                again(V.tensor_single_scalar(a.bitcast(I32), v.bitcast(I32), 1, ALU.arith_shift_right))
                again(V.tensor_scalar(y.bitcast(I32), a.bitcast(I32), -1.0, float(0x5F3759DF), ALU.mult, ALU.add))
                for it in range(3):
                    again(V.scalar_tensor_tensor(out=a, in0=y, scalar=-0.5, in1=y, op0=ALU.mult, op1=ALU.mult))
                    again(V.tensor_tensor(a, a, v, ALU.mult))
                    ins = V.scalar_tensor_tensor(out=y if it < 2 else dst, in0=a, scalar=1.5, in1=y,
                                                 op0=ALU.add, op1=ALU.mult)
                    if it < 2 or done is None:
                        again(ins)
                    else:
                        ins.then_inc(done, 1)

            dve.wait_ge(const_in, CONSTS)
            before = None
            for step in order:
                k, r = step[0], step[1:]
                if k not in DVE_KINDS or step[:2] == ("zE", 1):
                    continue
                if before:
                    dve.wait_ge(vector_done[before[0]], nth[before] + 1)
                before = step
                done = vector_done[k]
                if k == "ones":
                    V.tensor_copy(latg[:, 0:5], cols_in[:, 40:45])
                    V.memset(latg[:, 5:6], 1.0)
                    V.tensor_copy(small[:, :], gate_bc[:, 0:640])
                    V.memset(ones[:, :], 1.0).then_inc(done, 1)
                elif k == "adaA":
                    l, cc = r
                    if cc == 0 and l == 0:
                        dve.wait_ge(scalar_done["csilu"], nth["csilu",] + 1)
                    s_no = stage_no[step]
                    dve.wait_ge(stage_in[s_no % 2], stage_value[s_no])
                    par = nth[step] % 2
                    if nth[step] >= 2:
                        dve.wait_ge(filled, filled_at["adaM", *order_at["adaA", nth[step] - 2][1:]])
                    a = acc[:, par, :]
                    w = stage[s_no % 2][:, 0:KD * CW].rearrange("p (k w) -> p k w", k=KD)
                    again(V.tensor_scalar(a, w[:, 0, :], ccol[:, 0:1], None, ALU.mult))
                    for kk in range(1, KD):
                        again(V.scalar_tensor_tensor(out=a, in0=w[:, kk, :], scalar=ccol[:, kk:kk + 1], in1=a,
                                                     op0=ALU.mult, op1=ALU.add))
                    V.tensor_tensor(acc[0:1, par, :], acc[0:1, par, :], bias_row[:, s_no % 2, :], ALU.add)\
                        .then_inc(done, 1)
                elif k == "adaE":
                    l, cc = r
                    dve.wait_ge(filled, filled_at["adaM", l, cc])
                    b = bank_of("adaM", l, cc)
                    if cc < 4:
                        ins = V.tensor_copy(shift[:, l, 2 * cc:2 * cc + 2], b[:, 0:2])
                    elif cc < 8:
                        at = slice(2 * cc - 8, 2 * cc - 6)
                        ins = V.scalar_tensor_tensor(out=amp[:, l, at], in0=b[:, 0:2], scalar=1.0, in1=ng[:, l, at],
                                                     op0=ALU.add, op1=ALU.mult)
                    else:
                        ins = V.tensor_copy(gate_bc[:, CW * (cc - 8):CW * (cc - 7)], b[:, 0:CW])
                    ins.then_inc(done, 1)
                elif k == "rs":
                    l, half = r
                    at = slice(4 * half, 4 * half + 4)
                    dve.wait_ge(scalar_done["xsq"], nth["xsq", l, 4 * half + 3] + 1)
                    again(V.tensor_scalar(nt[:, 0, 0:4], ssq[:, at], 1.0 / D, EPS, ALU.mult, ALU.add))
                    inverse_root(rstd[:, at], nt[:, 0, 0:4], 4, done)
                    dve.wait_ge(vector_done[k], nth[step] + 1)
                elif k == "xh":
                    l, i = r
                    V.tensor_scalar(xhat[:, i, :].rearrange("p (a d) -> p a d", a=2), rows[:, :, i, :],
                                    rstd[:, i:i + 1], None, ALU.mult).then_inc(done, 1)
                elif k == "hx":
                    l, kk, half = r
                    dve.wait_ge(scalar_done[k], nth[step] + 1)
                    src = hx_tmp[nth[step] % 2]
                    at = slice(512 * half, 512 * half + 512)
                    again(V.tensor_copy(hT[0][:, kk, at], src[:, :]))
                    V.tensor_tensor(hT[1][:, kk, at], src[:, :], hT[0][:, kk, at].bitcast(F32), ALU.subtract)\
                        .then_inc(done, 1)
                elif k == "kvgE":
                    i = r[0]
                    dve.wait_ge(scalar_done[k], nth[step] + 1)
                    b = bank_of("kvg", i)
                    rotate(kn[:, i, :].rearrange("p (n d) -> p n d", d=64), b[:, 0:P].rearrange("p (n d) -> p n d", d=64), i, 2)
                    V.tensor_tensor(vs[1][:, i, :], b[:, 128:256], vs[0][:, i, :].bitcast(F32), ALU.subtract)\
                        .then_inc(done, 1)
                elif k == "sqE":
                    g, i = r
                    dve.wait_ge(filled, filled_at["sq", g, i])
                    b = bank_of("sq", g, i)
                    dst = rows[:, 1, i, :].rearrange("p (a q d) -> p a q d", q=2, d=64)[:, :, g, :]
                    rotate(dst, b[:, 0:CW].rearrange("p (n d) -> p n d", d=64), i, 4, done)
                elif k == "pqE":
                    i = r[0]
                    dve.wait_ge(filled, filled_at["pq", i])
                    b = bank_of("pq", i)
                    if i >= 2:
                        dve.wait_ge(qrot_out[i % 2], 16 * (i // 2))
                    rotate(cp[:, i % 2, 0:512].rearrange("p (n d) -> p n d", d=64),
                           b[:, :].rearrange("p (n d) -> p n d", d=64), i, 8, done)
                elif k in ("kTE", "aqTE", "apTE", "yTE", "qrTE", "pqTE", "pkTE", "pvE", "mpTE", "cTE"):
                    dve.wait_ge(scalar_done[k], nth[step] + 1)
                    b = shaped(bank_of(k[:-1], *r), step)
                    hi, lo = split_dst(step)
                    if k == "cTE":
                        V.scalar_tensor_tensor(out=lo, in0=b, scalar=latg[:, r[0]:r[0] + 1], in1=hi.bitcast(F32),
                                               op0=ALU.mult, op1=ALU.subtract).then_inc(done, 1)
                    else:
                        V.tensor_tensor(lo, b, hi.bitcast(F32), ALU.subtract).then_inc(done, 1)
                elif k == "gTE":
                    half = r[0]
                    if half == 0:
                        dve.wait_ge(even_in, EVEN_CONSTS)
                    dve.wait_ge(filled, filled_at["gT", half])
                    for m in range(2):
                        ins = V.tensor_scalar(grow(m)[:, 512 * half:512 * half + 512],
                                              bank_of("gT", half, m=m)[0:M_HEADS, :], gate_b_col[:, m:m + 1], None, ALU.add)
                    ins.then_inc(done, 1)
                elif k == "rowsA":
                    dve.wait_ge(vector_done["gTE"], nth["gTE", 1] + 1)
                    V.scalar_tensor_tensor(out=grow(2), in0=grow(1), scalar=-1.0, in1=grow(1), op0=ALU.mult, op1=ALU.min)\
                        .then_inc(done, 1)
                    again(V.memset(negM[:, :], 1.0))
                    again(V.memset(negM[:, :].rearrange("h (t s) -> h t s", s=P)[:, :, 0:1], 0.0))
                elif k == "rows":
                    dve.wait_ge(scalar_done["rowsB"], nth["rowsB",] + 1)
                    i_row, f_row, b_row = grow(0), grow(1), grow(2)
                    again(V.scalar_tensor_tensor(out=f_row, in0=f_row, scalar=0.0, in1=b_row, op0=ALU.min, op1=ALU.subtract))
                    again(V.tensor_tensor_scan(b_row, negM[:, :], f_row, 0.0, ALU.mult, ALU.add))
                    again(V.tensor_tensor(i_row, i_row, b_row, ALU.subtract))
                    again(V.memset(negM[:, :], 0.0))
                    tiles = lambda a: a.rearrange("h (t s) -> h t s", s=P)
                    again(V.tensor_copy(tiles(negM[:, :])[:, 1:T, 0:1], tiles(b_row)[:, 0:T - 1, P - 1:P]))
                    again(V.tensor_tensor_scan(f_row, negM[:, :], i_row, 0.0, ALU.add, ALU.max))
                    again(V.tensor_tensor(b_row, b_row, f_row, ALU.add))
                    V.tensor_scalar(negM[:, :], f_row, -1.0, None, ALU.mult).then_inc(done, 1)
                elif k == "asm":
                    i, g, ap = r
                    dve.wait_ge(filled, filled_at["asc", *r])
                    at = 0 if i else P
                    st = sst[:, nth[step] % 4, :]
                    if nth[step] >= 4:
                        pass
                    src = bank_of("asc", *r)[:, :].rearrange("p (j k) -> p j k", j=2)[:, :, at:256]
                    head = 4 * g + 2 * ap
                    again(V.tensor_reduce(st[:, 0:2], src, AX, ALU.max))
                    again(V.scalar_tensor_tensor(out=st[:, 0:2], in0=st[:, 0:2], scalar=S_SCALE, in1=sink_bc[:, head:head + 2],
                                                 op0=ALU.mult, op1=ALU.max))
                    V.tensor_scalar(st[:, 2:4], st[:, 0:2], -1.0, None, ALU.mult)
                    V.tensor_tensor(st[:, 4:6], sink_bc[:, head:head + 2], st[:, 0:2], ALU.subtract).then_inc(done, 1)
                elif k == "ano":
                    i, g, ap = r
                    st = sst[:, nth["asm", i, g, ap] % 4, :]
                    dve.wait_ge(scalar_done["asm"], nth["asm", *r] + 1)
                    again(V.tensor_tensor(st[:, 8:10], st[:, 4:6], st[:, 6:8], ALU.add))
                    again(V.reciprocal(st[:, 10:12], st[:, 8:10]))
                    dve.wait_ge(filled, filled_at["apv", *r])
                    col = 64 * (4 * g + 2 * ap)
                    V.tensor_tensor(rows[:, 1, i, col:col + P].rearrange("p (j d) -> p j d", j=2),
                                    bank_of("apv", *r)[:, 0:P].rearrange("p (j d) -> p j d", j=2),
                                    st[:, 10:12].unsqueeze(2).broadcast_to([P, 2, 64]), ALU.mult).then_inc(done, 1)
                elif k == "colsE":
                    dve.wait_ge(filled, filled_at["colsT",])
                    b = bank_of("colsT")
                    again(V.tensor_copy(mcols[:, :], b[:, 0:160]))
                    V.tensor_copy(gcol[:, :, :], mcols[:, 0:32].rearrange("p (t h) -> p t h", h=4))
                    nm = mcols[:, 32:64].rearrange("p (t h) -> p t h", h=4)
                    mm = mcols[:, 64:96].rearrange("p (t h) -> p t h", h=4)
                    m_end = mcols[:, 96:128].rearrange("p (h t) -> p t h", h=4)
                    nM_end = mcols[:, 128:160].rearrange("p (h t) -> p t h", h=4)
                    V.tensor_copy(margs[:, 0, 0, :], nm[:, 0, :])
                    V.tensor_tensor(margs[:, 0, 1:T, :], nm[:, 1:T, :], m_end[:, 0:T - 1, :], ALU.add)
                    V.tensor_tensor(margs[:, 1, :, :], mcols[:, 0:32].rearrange("p (t h) -> p t h", h=4), nM_end, ALU.add)
                    V.tensor_copy(margs[:, 2, 0, :], nM_end[:, 0, :])
                    V.tensor_tensor(margs[:, 2, 1:T, :], nM_end[:, 1:T, :], m_end[:, 0:T - 1, :], ALU.add)
                    V.tensor_scalar(margs[:, 3, :, :], mm, -1.0, None, ALU.mult).then_inc(done, 1)
                elif k == "cols":
                    dve.wait_ge(filled, filled_at["apv", T - 1, 1, 1])
                    dve.wait_ge(vector_done["ano"], nth["ano", T - 1, 1, 1] + 1)
                    V.memset(raw[:, 0:3], 0.0)
                    for b in range(2):
                        V.memset(vm[b][0][:, :, M_DV + 1:VW].bitcast(F32), 0.0)
                        V.memset(vm[b][1][:, :, M_DV:VW].bitcast(F32), 0.0)
                    for b in range(2):
                        ins = V.memset(vm[b][0][:, :, M_DV:M_DV + 1].bitcast(F32), 1.0)
                    ins.then_inc(done, 1)
                elif k == "conv":
                    p, which = r
                    dve.wait_ge(scalar_done["mqkE"], nth["mqkE", p, which, 1] + 1)
                    if which:
                        dve.wait_ge(vector_done["qksp"], nth["qksp", p, 0] + 1)
                    elif p:
                        dve.wait_ge(filled, filled_at["kN", p - 1, T - 2])
                    w = cw[:, 2 * which + p, :]
                    again(V.tensor_scalar(cacc[:, :], raw[:, 0:S], w[:, 0:1], None, ALU.mult))
                    for t in range(1, CONV_K):
                        ins = V.scalar_tensor_tensor(out=cacc[:, :], in0=raw[:, t:t + S], scalar=w[:, t:t + 1],
                                                     in1=cacc[:, :], op0=ALU.mult, op1=ALU.add)
                        if t < CONV_K - 1:
                            again(ins)
                    ins.then_inc(done, 1)
                elif k == "qksp":
                    p, which = r
                    dve.wait_ge(scalar_done["silu"], nth["silu", p, which] + 1)
                    hi, lo = kmT if which else qmT
                    V.scalar_tensor_tensor(out=lo[:, :], in0=cacc[:, :], scalar=M_SCALE if which else 1.0,
                                           in1=hi[:, :].bitcast(F32), op0=ALU.mult, op1=ALU.subtract).then_inc(done, 1)
                elif k == "mSE":
                    p, i = r
                    dve.wait_ge(scalar_done["mBE"], nth["mBE", p, i] + 1)
                    dve.wait_ge(filled, filled_at["mS", p, i])
                    for j in range(2):
                        last = V.tensor_tensor(dtmp[:, j * P:(j + 1) * P], bank_of("mS", p, i, m=j)[:, 0:P],
                                               Wt[:, nth[step] % 2, j, :], ALU.mult)
                    again(last)
                    if nth[step]:
                        dve.wait_ge(filled, filled_at["mO", *order_at["mSE", nth[step] - 1][1:]])
                    flat = lambda a: a[:, :, :].rearrange("p j t -> p (j t)")
                    again(V.tensor_copy(flat(sw[0]), dtmp[:, 0:2 * P]))
                    V.tensor_tensor(flat(sw[1]), dtmp[:, 0:2 * P], flat(sw[0]).bitcast(F32), ALU.subtract).then_inc(done, 1)
                elif k == "kNE":
                    p, i = r
                    dve.wait_ge(filled, filled_at["kN", p, i])
                    if i == 0 and p == 0:
                        dve.wait_ge(scalar_done["cols"], nth["cols",] + 1)
                    ws_ = margs[:, 1, i, 2 * p:2 * p + 2].unsqueeze(2).broadcast_to([P, 2, 64])
                    again(V.scalar_tensor_tensor(out=dtmp[:, 256:384].rearrange("p (j d) -> p j d", j=2),
                                                 in0=bank_of("kN", p, i)[:, 0:P].rearrange("p (j d) -> p j d", j=2),
                                                 scalar=M_SCALE, in1=ws_, op0=ALU.mult, op1=ALU.mult))
                    if nth[step]:
                        dve.wait_ge(filled, filled_at["mC", *order_at["kNE", nth[step] - 1][1:]])
                    again(V.tensor_copy(kw[0][:, :], dtmp[:, 256:384]))
                    V.tensor_tensor(kw[1][:, :], dtmp[:, 256:384], kw[0][:, :].bitcast(F32), ALU.subtract).then_inc(done, 1)
                elif k == "mOE":
                    p, i = r
                    dve.wait_ge(filled, filled_at["mO", p, i])
                    for j in range(2):
                        h = 2 * p + j
                        b = bank_of("mO", p, i, m=j)
                        y = rows[:, 0, i, M_DV * h:M_DV * (h + 1)]
                        if i:
                            V.tensor_copy(htile[:, :], b[:, 0:VW]).then_inc(dve_step, 1)
                            steps_done[0] += 1
                            dve.wait_ge(dve_step, steps_done[0])
                            V.scalar_tensor_tensor(out=y, in0=b[:, 256:256 + M_DV], scalar=margs[:, 0, i, h:h + 1],
                                                   in1=htile[:, 0:M_DV], op0=ALU.mult, op1=ALU.add)
                            last = V.scalar_tensor_tensor(out=mden[:, i, h:h + 1], in0=b[:, 256 + M_DV:257 + M_DV],
                                                          scalar=margs[:, 0, i, h:h + 1], in1=htile[:, M_DV:M_DV + 1],
                                                          op0=ALU.mult, op1=ALU.add)
                            if j == 0:
                                again(last)
                        else:
                            V.tensor_copy(y, b[:, 0:M_DV])
                            last = V.tensor_copy(mden[:, i, h:h + 1], b[:, M_DV:M_DV + 1])
                    last.then_inc(done, 1)
                elif k == "mCE":
                    p, i = r
                    dve.wait_ge(filled, filled_at["mC", p, i])
                    b = bank_of("mC", p, i)
                    for j in range(2):
                        part = slice(64 * j, 64 * j + 64)
                        src = b[part, 256 * j:256 * j + VW]
                        if i == 0:
                            last = V.tensor_copy(Cst[part, :], src)
                        else:
                            last = V.scalar_tensor_tensor(out=Cst[part, :], in0=Cst[part, :],
                                                          scalar=margs[part, 2, i, 2 * p + j:2 * p + j + 1], in1=src,
                                                          op0=ALU.mult, op1=ALU.add)
                    again(last)
                    again(V.tensor_copy(Csp[0][:, :], Cst[:, :]))
                    V.tensor_tensor(Csp[1][:, :], Cst[:, :], Csp[0][:, :].bitcast(F32), ALU.subtract).then_inc(done, 1)
                elif k == "mfin":
                    dve.wait_ge(scalar_done["hsq"], nth["hsq", 1, T - 1] + 1)
                    f = lambda a: a[:, :, :].rearrange("p t h -> p (t h)")
                    floor = margs[:, 3, :, :].rearrange("p t h -> p (t h)")
                    again(V.scalar_tensor_tensor(out=f(mden), in0=f(mden), scalar=-1.0, in1=f(mden), op0=ALU.mult, op1=ALU.max))
                    again(V.tensor_tensor(f(mden), f(mden), floor, ALU.max))
                    again(V.reciprocal(f(mden), f(mden)))
                    again(V.tensor_tensor(f(hss), f(hss), f(mden), ALU.mult))
                    again(V.tensor_tensor(f(hss), f(hss), f(mden), ALU.mult))
                    again(V.tensor_scalar(nt[:, 0, :], f(hss), 1.0 / M_DV, EPS, ALU.mult, ALU.add))
                    inverse_root(f(msc_t), nt[:, 0, :], 32, None)
                    V.scalar_tensor_tensor(out=f(msc_t), in0=f(msc_t), scalar=0.5, in1=f(mden), op0=ALU.mult, op1=ALU.mult)\
                        .then_inc(done, 1)
                    dve.wait_ge(vector_done[k], nth[step] + 1)
                elif k == "mscale":
                    i = r[0]
                    for h in range(M_HEADS):
                        y = rows[:, 0, i, M_DV * h:M_DV * (h + 1)]
                        last = V.scalar_tensor_tensor(out=y, in0=y, scalar=msc_t[:, i, h:h + 1],
                                                      in1=hg[:, M_DV * h:M_DV * (h + 1)], op0=ALU.mult, op1=ALU.mult)
                    last.then_inc(done, 1)
                elif k == "moE":
                    p, i = r
                    dve.wait_ge(scalar_done[k], nth[step] + 1)
                    dve.wait_ge(vector_done["mscale"], nth["mscale", i] + 1)
                    y = rows[:, 0, i, CW * p:CW * (p + 1)]
                    par = gate_no[step] % 2
                    V.scalar_tensor_tensor(out=y, in0=tmp[:, CW * par:CW * (par + 1)], scalar=1.0, in1=y,
                                           op0=ALU.add, op1=ALU.mult).then_inc(done, 1)
                elif k == "zE":
                    l, zc, i = r
                    if l == 1:
                        continue
                    dve.wait_ge(scalar_done[k], nth[step] + 1)
                    if zc < 2:
                        dve.wait_ge(vector_done["moE"], nth["moE", zc, i] + 1)
                    y = rows[:, zc // 2, i, CW * (zc % 2):CW * (zc % 2 + 1)]
                    par = gate_no[step] % 2
                    V.tensor_tensor(y, tmp[:, CW * par:CW * (par + 1)], y, ALU.mult).then_inc(done, 1)
                elif k == "poE":
                    l, oc, i = r
                    dve.wait_ge(filled, filled_at["po", l, oc, i])
                    if oc == 0:
                        dve.wait_ge(x_in[i], 16 * (l + 2))
                        dve.wait_ge(vector_done["adaE"], nth["adaE", l, 11] + 1)
                    t = dtmp[:, CW * (nth[step] % 2):CW * (nth[step] % 2 + 1)]
                    again(V.tensor_tensor(t, bank_of("po", l, oc, i)[:, 0:CW], gate_bc[:, CW * oc:CW * (oc + 1)], ALU.mult))
                    y = rows[:, oc // 2, i, CW * (oc % 2):CW * (oc % 2 + 1)]
                    V.tensor_tensor(y, y, t, ALU.add).then_inc(done, 1)
                elif k == "lrs":
                    dve.wait_ge(scalar_done["lsq"], nth["lsq", T - 1] + 1)
                    V.tensor_scalar(nt[:, 0, 0:T], ssq[:, 0:T], 1.0 / C_QL, EPS, ALU.mult, ALU.add)
                    again(V.tensor_scalar(nt[:, 0, T:2 * T], ssq[:, T:2 * T], 1.0 / C_KVL, EPS, ALU.mult, ALU.add))
                    inverse_root(rstd[:, 0:2 * T], nt[:, 0, 0:2 * T], 2 * T, done)
                    dve.wait_ge(vector_done[k], nth[step] + 1)
                elif k == "lsc":
                    i = r[0]
                    V.tensor_scalar(craw[:, i, 0:C_QL], craw[:, i, 0:C_QL], rstd[:, i:i + 1], None, ALU.mult)
                    V.tensor_scalar(craw[:, i, C_QL:O_KR], craw[:, i, C_QL:O_KR], rstd[:, T + i:T + i + 1], None, ALU.mult)
                    kr = craw[:, i:i + 1, O_KR:O_KR + 64]
                    again(rotate(craw[:, i:i + 1, O_KR + 64:CRW], kr, i, 1))
                    V.tensor_copy(kr, craw[:, i:i + 1, O_KR + 64:CRW]).then_inc(done, 1)
                elif k == "msm":
                    h, i = r
                    st = cst[:, nth[step] % 4, :]
                    n = i // 4 + 1
                    for b in range(n):
                        dve.wait_ge(filled, filled_at["msc", h, i, b])
                        nk = min(512, P * (i + 1) - 512 * b)
                        last = V.tensor_reduce(st[:, b:b + 1], bank_of("msc", h, i, b)[:, 0:nk], AX, ALU.max)
                    again(last)
                    if n == 2:
                        again(V.tensor_tensor(st[:, 0:1], st[:, 0:1], st[:, 1:2], ALU.max))
                    V.tensor_scalar(st[:, 2:3], st[:, 0:1], -C_SCALE, None, ALU.mult).then_inc(done, 1)
                elif k == "mno":
                    h, i = r
                    st = cst[:, nth["msm", h, i] % 4, :]
                    dve.wait_ge(scalar_done["msm"], nth["msm", h, i] + 1)
                    s_ = st[:, 3:4]
                    if i >= 4:
                        again(V.tensor_tensor(st[:, 3:4], st[:, 3:4], st[:, 4:5], ALU.add))
                    again(V.reciprocal(st[:, 5:6], st[:, 3:4]))
                    dve.wait_ge(filled, filled_at["mpv", h, i, i // 4])
                    if h % 2 == 0:
                        dve.wait_ge(scalar_done["zE"], nth["zE", 1, h // 2, i] + 1)
                    y = rows[:, h // 4, i, (h % 4) * P:(h % 4 + 1) * P]
                    V.scalar_tensor_tensor(out=y, in0=bank[job["mpv", h, i, 0] % NPSUM][:, 0:P], scalar=st[:, 5:6], in1=y,
                                           op0=ALU.mult, op1=ALU.mult).then_inc(done, 1)
                elif k == "fin":
                    i = r[1]
                    if i == 0:
                        dve.wait_ge(final_in, 16)
                    V.scalar_tensor_tensor(out=xhat[:, i, :].rearrange("p (a d) -> p a d", a=2), in0=rows[:, :, i, :],
                                           scalar=rstd[:, i:i + 1], in1=final_bc[:, :].rearrange("p (a d) -> p a d", a=2),
                                           op0=ALU.mult, op1=ALU.mult).then_inc(done, 1)
                else:
                    raise ValueError(k)


_INS = ["x", "ada_w", "ada_b", "e_w_in", "e_head_g", "e_sinks", "e_w_out", "o_w_in", "o_w_uq", "o_w_ukv", "o_w_out",
        "final_g"]


def constants():
    import numpy as np

    inv = np.float32(1.0) / (np.float32(10000.0) ** (np.arange(0, S_HD, 2, dtype=np.float32) / np.float32(S_HD)))
    ang = np.arange(S, dtype=np.float32)[:, None] * inv[None, :]
    cos, sin = np.cos(ang), np.sin(ang)
    rope = np.concatenate([cos, cos, -sin, sin], axis=1).astype(np.float32)
    small = np.zeros((P, 640), np.float32)
    big = -(2.0 ** 100)
    small[:, 0:128] = np.eye(P)
    small[:, 128:256] = np.where(np.arange(P)[:, None] <= np.arange(P)[None, :], 0.0, big)
    for at in (0, 64):
        small[at, 256:320] = 1.0
        small[at + 1, 320:384] = 1.0
        small[at, 384:448] = big
        small[at, 576:640] = big
        small[at + 1, 384:512] = big
    return {"rope": rope, "ident": np.eye(P, dtype=np.float32), "small": small}


def kernel(**inputs):
    import numpy as _np
    import concourse.bacc as _bacc
    from concourse import mybir as _mybir
    from concourse.bass_utils import run_bass_kernel_spmd as _run

    nc = _bacc.Bacc("TRN2", target_bir_lowering=False, num_devices=1)
    arrays, args = {}, []
    for name in _INS:
        arrays["in_" + name] = _np.ascontiguousarray(inputs[name])
    arrays["in_columns"] = _np.ascontiguousarray(_np.concatenate(
        [_np.asarray(inputs[n]).reshape(-1, P) for n in ("c", "norm_g", "e_conv_w", "o_q_g", "o_kv_g")]).T)
    arrays["in_gate_b"] = _np.ascontiguousarray(_np.asarray(inputs["e_gate_b"]).reshape(2, M_HEADS).T)
    for name, value in constants().items():
        arrays["const_" + name] = value
    for name, a in arrays.items():
        if name == "in_x":
            a = arrays[name] = a.reshape(S, D)
        args.append(nc.dram_tensor(name, a.shape, _mybir.dt.from_np(a.dtype), kind="ExternalInput").ap())
    args.append(nc.dram_tensor("out_0", (1, S, D), F32, kind="ExternalOutput").ap())
    trunk(nc, *args)
    r = _run(nc, [arrays], core_ids=[0])
    return r.results[0]["out_0"]
```

```python
from contextlib import ExitStack

import concourse.bass as bass
from concourse import mybir

F32 = mybir.dt.float32
F32R = mybir.dt.float32r
BF16 = mybir.dt.bfloat16
I32 = mybir.dt.int32
ALU = mybir.AluOpType
ACT = mybir.ActivationFunctionType
AX = mybir.AxisListType.X

P = 128
S, D = 1024, 1024
T = S // P
KD = D // P
CW = 256
EPS = 1e-6
M_HEADS, M_DQK, M_DV, CONV_K = 4, 64, 128, 4
S_QH, S_KVH, S_HD = 8, 2, 64
S_G = S_QH // S_KVH
C_HEADS, C_QL, C_KVL, C_NOPE, C_ROPE, C_DV = 8, 384, 256, 128, 64, 128
KQ, KKV = C_QL // P, C_KVL // P
M_SCALE = M_DQK ** -0.5
S_SCALE = S_HD ** -0.5
C_SCALE = (C_NOPE + C_ROPE) ** -0.5
VW = M_DV + 2
E_Q, E_K, E_V, E_O, E_IF = 0, 256, 512, 1024, 1536
E_SQ, E_SK, E_SV, E_Z = 1544, 2056, 2184, 2312
O_CQ, O_CKV, O_KR, O_Z = 0, 384, 640, 704
CRW = 768
FLAT = 2112
NPSUM = 8
CPT = 4
SPLITS = ("kTE", "aqTE", "apTE", "yTE", "qrTE", "pqTE", "pkTE", "pvE", "mpTE", "cTE")
ACT_KINDS = frozenset(("csilu", "ws", "xsq", "hx", "kvgE", "rowsB", "aex", "cols", "mqkE", "silu", "mvE", "vsp", "mBE",
                       "hsq", "moE", "zE", "latE", "lsq", "mex") + SPLITS)
DVE_KINDS = frozenset(("ones", "adaA", "adaP", "adaE", "rs", "xh", "hx", "kvgE", "sqE", "pqE", "gTE", "rowsA", "rows", "asm",
                       "ano", "colsE", "cols", "conv", "qksp", "mSE", "kNE", "mOE", "mCE", "mfin", "mscale", "moE",
                       "zE", "poE", "lrs", "lsc", "msm", "mno", "fin") + SPLITS)


def chunks():
    c = {}
    c["kvg"] = [(0, KD, 264, [("e_in", E_SK, 128, 0), ("e_in", E_SV, 128, 128), ("e_in", E_IF, 8, 256)])]
    for g in range(2):
        c["sq", g] = [(0, KD, CW, [("e_in", E_SQ + CW * g, CW, 0)])]
    for p in range(2):
        c["mqk", p] = [(0, KD, CW, [("e_in", E_Q + P * p, P, 0), ("e_in", E_K + P * p, P, P)])]
        c["mv", p] = [(0, KD, CW, [("e_in", E_V + CW * p, CW, 0)])]
        c["mo", p] = [(0, KD, CW, [("e_in", E_O + CW * p, CW, 0)])]
    for z in range(4):
        c["z", 0, z] = [(0, KD, CW, [("e_in", E_Z + CW * z, CW, 0)])]
        c["z", 1, z] = [(0, KD, CW, [("o_in", O_Z + CW * z, CW, 0)])]
        c["out", 0, z] = [(0, KD, CW, [("e_out", CW * z, CW, 0)])]
        c["out", 1, z] = [(0, KD, CW, [("o_out", CW * z, CW, 0)])]
    c["lat", 0] = [(0, KD, CW, [("o_in", 0, CW, 0)])]
    c["lat", 1] = [(0, KD, CW, [("o_in", CW, CW, 0)])]
    c["lat", 2] = [(0, KD, 192, [("o_in", 2 * CW, 192, 0)])]
    c["uqr"] = [(0, KQ, 512, [("uq", 192 * h + C_NOPE, C_ROPE, C_ROPE * h) for h in range(C_HEADS)])]
    for a in range(C_HEADS // 2):
        c["hp", a] = [(0, KQ, 256, [("uq", 192 * (2 * a + j), P, P * j) for j in range(2)]),
                      (768, KKV, 512, [("ukv", 512 * a, 512, 0)])]
    return c


CHUNKS = chunks()
LAT_W = {0: CW, 1: CW, 2: 192}


def ada_part(l, c, q):
    return [("adaP", l, c, q)] if q else [("adaA", l, c)]


def with_ada(steps, *lc):
    part = len(steps) // 4
    out = steps[:2]
    for q in range(4):
        out += ada_part(*lc, q) + steps[2 + q * part:2 + (q + 1) * part]
    return out + steps[2 + 4 * part:] + [("adaM", *lc), ("adaE", *lc)]


def spread(a, b):
    out, n = [], 0
    for i, step in enumerate(a):
        out.append(step)
        while n < len(b) * (i + 1) // len(a):
            out.append(b[n])
            n += 1
    return out + b[n:]


def proj(kind, *key):
    out = []
    for i in range(T + 1):
        if i < T:
            out.append((kind, *key, i))
        if i >= 1:
            out.append((kind + "E", *key, i - 1))
    return out


def window_attention():
    units = [(i, g, ap) for i in range(T) for ap in range(2) for g in range(2)]
    at = {2: (0, 10), 8: (0, 11), 14: (1, 0), 20: (1, 1), 26: (1, 2)}
    n, o = len(units), []
    for t in range(n + 6):
        unit = lambda lag: [units[t - lag]] if 0 <= t - lag < n else []
        for u in unit(0):
            if t == 0:
                o += [("aqT", 0, 0), ("aqTE", 0, 0), ("aqT", 0, 1), ("aqTE", 0, 1)]
            o.append(("asc", *u))
        o += [("asm", *u) for u in unit(1)]
        o += [("aex", *u) for u in unit(1)]
        o += [("ano", *u) for u in unit(4)]
        for u in unit(2):
            o += [("apT", *u), ("apTE", *u)]
        o += [("apv", *u) for u in unit(3)]
        for i, g, ap in unit(0):
            if g == 1 and i < T - 1:
                o += [("aqT", i + 1, ap), ("aqTE", i + 1, ap)]
        for q in range(4):
            if t - q in at:
                o += ada_part(*at[t - q], q)
        if t - 5 in at:
            o += [("adaM", *at[t - 5]), ("adaE", *at[t - 5])]
    return o


def memory_cells(p):
    o = []
    for t in range(T + 2):
        if 1 <= t < T:
            o.append(("mC", p, t - 1))
        if t < T:
            o += [("vsp", p, t), ("mB", p, t)]
        if 1 <= t < T:
            o.append(("mCE", p, t - 1))
        if t < T - 1:
            o.append(("kN", p, t))
        if t < T:
            o.append(("mS", p, t))
        if 2 <= t <= T + 1:
            o.append(("mOE", p, t - 2))
        if 1 <= t <= T:
            o.append(("mO", p, t - 1))
        if t < T - 1:
            o.append(("kNE", p, t))
        if t < T:
            o += [("mBE", p, t), ("mSE", p, t)]
        if 2 <= t <= T + 1:
            o.append(("hsq", p, t - 2))
    return o + [("mfin", p)]


def memory_inputs(p):
    o = []
    for which in range(2):
        for half in range(2):
            o += [("mqk", p, which, half), ("mqkE", p, which, half)]
        o += [("conv", p, which), ("silu", p, which), ("qksp", p, which)]
    return o


def latent_attention():
    def turned(what, h, half):
        return [(what, h, half), (what + "E", h, half)]

    def early(h):
        return ([("ql", h // 2)] + turned("qrT", h // 2, 0) if h % 2 == 0 else []) + turned("pqT", h, 0)

    def late(h):
        return ((turned("qrT", h // 2, 1) if h % 2 == 0 else []) + turned("pqT", h, 1)
                + turned("pkT", h, 0) + turned("pkT", h, 1))

    units = [(h, i) for h in range(C_HEADS) for i in range(T)]
    n, o = len(units), []
    for t in range(n + 6):
        unit = lambda lag: [units[t - lag]] if 0 <= t - lag < n else []
        o += [("msm", *u) for u in unit(1)]
        o += [("mex", *u) for u in unit(1)]
        o += [("mno", *u) for u in unit(4)]
        for h, i in unit(0):
            if i == 0:
                if h:
                    o += late(h)
                else:
                    for what in ("pqT", "pkT", "pv"):
                        o += turned(what, 0, 0) + turned(what, 0, 1)
                    o += [("ql", 0)] + turned("qrT", 0, 0) + turned("qrT", 0, 1)
            if i:
                o += [("msc", h, i, b) for b in range(i // 4 + 1)]
        for h, i in unit(2):
            for b in range(i // 4 + 1):
                o += [("mpT", h, i, b), ("mpTE", h, i, b)]
        for h, i in unit(3):
            if i == 0 and h:
                for half in range(2):
                    o += [("pv", h, half), ("pvE", h, half)]
            o += [("mpv", h, i, b) for b in range(i // 4 + 1)]
        for h, i in unit(0):
            if i == 0:
                o.append(("msc", h, 0, 0))
            if i == 5 and h + 1 < C_HEADS:
                o += early(h + 1)
    return o


def plan():
    o = []

    def norm(l, half):
        for i in range(4 * half, 4 * half + 4):
            o.append(("xsq", l, i))
        o.append(("rs", l, half))
        for i in range(4 * half, 4 * half + 4):
            o.append(("xh", l, i))

    def last_norm(half):
        for i in range(4 * half, 4 * half + 4):
            o.append(("xsq", 2, i))
        if half == 0:
            o.append(("fg",))
        o.append(("rs", 2, half))
        for i in range(4 * half, 4 * half + 4):
            o.append(("fin", 2, i))

    def hidden(l):
        for half in range(2):
            for k in range(KD + 1):
                if k < KD:
                    o.append(("xT", l, k, half))
                if k:
                    o.append(("hx", l, k - 1, half))

    def out_layer(l):
        for half in range(2):
            for k in range(KD + 1):
                if k < KD:
                    o.append(("yT", l, k, half))
                if k:
                    o.append(("yTE", l, k - 1, half))
            for i in range(4 * half, 4 * half + 4):
                o.append(("xl", l + 2, i))
        for oc in range(4):
            for step in proj("po", l, oc):
                o.append(step)
                if step in (("poE", l, 3, 3), ("poE", l, 3, 7)):
                    half = step[3] // 4
                    if l == 0:
                        o.extend(("xs", i) for i in range(4 * half, 4 * half + 4))
                        norm(1, half)
                    else:
                        last_norm(half)

    o += [("ones",), ("csilu",)]
    for c in range(8):
        for q in range(4):
            o += ada_part(0, c, q)
        if c:
            o += [("adaM", 0, c - 1), ("adaE", 0, c - 1)]
        if c == 3:
            norm(0, 0)
        if c == 6:
            norm(0, 1)
    o += [("adaM", 0, 7), ("adaE", 0, 7)]
    hidden(0)
    o += with_ada(proj("kvg"), 0, 8)
    for half in range(2):
        o += [("gT", half), ("gTE", half), ("kT", half), ("kTE", half)]
    o += [("rowsA",), ("rowsB",), ("rows",)]
    o += with_ada(proj("sq", 0) + proj("sq", 1), 0, 9)
    o += window_attention()
    o += [("colsT",), ("colsE",), ("cols",)]
    o += memory_inputs(0)
    o += with_ada(proj("mv", 0), 1, 3)
    o += spread(memory_cells(0), proj("z", 0, 2) + with_ada(proj("z", 0, 3), 1, 4))
    o += [("mscale", 0, i) for i in range(T)]
    o += memory_inputs(1)
    o += with_ada(proj("mv", 1), 1, 5)
    o += spread(memory_cells(1), proj("mo", 0) + with_ada(proj("z", 0, 0), 1, 6))
    o += [("mscale", 1, i) for i in range(T)]
    o += with_ada(proj("mo", 1), 1, 7)
    o += proj("z", 0, 1)
    out_layer(0)
    hidden(1)
    for c in range(3):
        o += with_ada(proj("lat", c), 1, 8 + c)
    for i in range(T):
        o.append(("lsq", i))
    o += with_ada(proj("z", 1, 0), 1, 11)
    o.append(("lrs",))
    o += spread(proj("z", 1, 1), [("lsc", i) for i in range(T)])
    for z in range(2, 4):
        o += proj("z", 1, z)
    for ks in (range(KQ), range(KQ, 6)):
        for half in range(2):
            for k in ks:
                o += [("cT", k, half), ("cTE", k, half)]
    for s in proj("pq"):
        o.append(s)
        if s[0] == "pqE":
            o.append(("qs", s[1]))
    o += latent_attention()
    out_layer(1)

    uses = {}
    for at, step in enumerate(o):
        if chunk_of(step) is not None:
            uses.setdefault(chunk_of(step), []).append(at)
    names = list(uses)
    ins = {uses[names[0]][0] - 40: [("ws", 0)]}
    for n in range(1, len(names)):
        at = uses[names[n - 1]][1] + 2
        if n >= 2:
            at = max(at, uses[names[n - 2]][-1] + 3)
        assert at <= uses[names[n]][0]
        ins.setdefault(at, []).append(("ws", n))
    final = []
    for at, step in enumerate(o):
        final += ins.get(at, []) + [step]
    stages = [s for s in final if s[0] in ("ws", "adaA")]
    out, n = [("wl", 0), ("cl", 0), ("wl", 1), ("xl", 0, 0), ("xl", 0, 1)], 2
    for step in final:
        out.append(step)
        if step[0] in ("ws", "adaA") and n < len(stages):
            out.append(("wl", n))
            if n < 5:
                out += [("xl", 0, 2 * n - 2), ("xl", 0, 2 * n - 1)]
            if n == 4:
                out.append(("cl", 1))
            n += 1
    return out, names, stages


def chunk_of(s):
    k = s[0]
    if k == "kvg":
        return "kvg"
    if k in ("sq", "mqk", "mv", "mo", "lat"):
        return s[0], s[1]
    if k == "z":
        return "z", s[1], s[2]
    if k == "po":
        return "out", s[1], s[2]
    if k == "pq":
        return "uqr"
    if k in ("pqT", "pkT", "pv"):
        return "hp", s[1] // 2
    return None


BANKS = {("mo", 1): tuple(range(NPSUM)), ("z", 1): tuple(range(NPSUM)),
         "asc": (0, 1, 2), "aqT": (3, 4), "apT": (3, 4), "apv": (6, 7),
         "z": (0, 1), "mo": (0, 1), "mB": (2,), "kN": (5,), "mC": (5,), "mS": (3, 4), "mO": (6, 7),
         "msc": (0, 1, 2, 3), "mpT": (4, 5), "qrT": (4, 5), "pqT": (4, 5), "pkT": (0, 1, 2, 3), "pv": (4, 5),
         "mpv": (6, 7)}


def freeing(step):
    k, r = step[0], step[1:]
    if k in ("adaM",):
        return ("adaE", *r), "dve"
    if k == "xT":
        return ("hx", *r), "act"
    if k in ("kvg", "sq", "kT", "gT", "aqT", "apT", "mS", "kN", "yT", "po", "cT", "pq",
             "qrT", "pqT", "pkT", "pv", "mpT", "mO", "mC"):
        return (k + "E", *r), "dve"
    if k == "colsT":
        return ("colsE",), "dve"
    if k in ("lat", "mqk", "mv", "mB", "mo", "z"):
        return (k + "E", *r), "act"
    if k == "asc":
        return ("aex", *r), "act"
    if k == "apv":
        return ("ano", *r), "dve"
    if k == "msc":
        return ("mex", *r[:2]), "act"
    if k == "mpv":
        return ("mno", *r[:2]), "dve"
    return None


def banks_of(step):
    if freeing(step) is None:
        return 0
    if step[0] in ("mS", "mO", "gT"):
        return 2
    if step[0] == "mpv":
        return 1 if step[3] == 0 else 0
    return 1


def trunk(nc, x, ada_w, ada_b, e_in, head_g, sinks, e_out, o_in, uq, ukv, o_out, final_g, columns, gate_b,
          rope, ident_in, small_in, out):
    order, chunk_names, stages = plan()
    nth, seen = {}, {}
    for s in order:
        nth[s] = seen.get(s[0], 0)
        seen[s[0]] = nth[s] + 1
    job, jobs = {}, []
    filled_at = {}
    for s in order:
        if banks_of(s):
            job[s] = len(jobs)
            jobs += [s] * banks_of(s)
    for s in order:
        if s[0] == "mpv":
            job[s] = job["mpv", s[1], s[2], 0]
    bank_no, before_in_bank, turn, holder = [], [], {}, {}
    place = {s: n for n, s in enumerate(order)}
    for n, s in enumerate(jobs):
        group = BANKS.get(s[:2], BANKS.get(s[0], tuple(range(NPSUM))))
        if s[0] == "adaM":
            read = [b for b in group if b not in holder or place[freeing(jobs[holder[b]])[0]] < place[s]]
            group = (min(read, key=lambda b: holder.get(b, -1)),)
        b = group[turn.get(group, 0) % len(group)]
        turn[group] = turn.get(group, 0) + 1
        before_in_bank.append(holder.get(b))
        bank_no.append(b)
        holder[b] = n
    for n, m in enumerate(before_in_bank):
        assert m is None or place[freeing(jobs[m])[0]] < place[jobs[n]], (jobs[m], jobs[n])
    fills = 0
    for s in order:
        if freeing(s) is None:
            continue
        if s[0] == "mpv":
            if s[3] == s[2] // 4:
                fills += 1
                for b in range(s[3] + 1):
                    filled_at["mpv", s[1], s[2], b] = fills
        else:
            fills += banks_of(s)
            filled_at[s] = fills
    chunk_no = {name: n for n, name in enumerate(chunk_names)}
    last_job = {}
    for s in order:
        if chunk_of(s) is not None:
            last_job[chunk_of(s)] = filled_at[s]
    mat = {"e_in": e_in, "e_out": e_out, "o_in": o_in, "o_out": o_out, "uq": uq, "ukv": ukv}
    stage_no = {s: n for n, s in enumerate(stages)}
    stage_value, per = [], [0, 0]
    for n, s in enumerate(stages):
        count = 2 if s[0] == "adaA" else sum(len(b[3]) for b in CHUNKS[chunk_names[s[1]]])
        per[n % 2] += 16 * count
        stage_value.append(per[n % 2])

    order_at = {(s[0], nth[s]): s for s in order}
    gate_steps = [s for s in order if s[0] == "moE" or s[:2] == ("zE", 0)]
    gate_no = {s: n for n, s in enumerate(gate_steps)}
    qr_dram = nc.dram_tensor("q_rot_scratch", (S, C_HEADS * C_ROPE), F32, kind="Internal").ap()
    x1_dram = nc.dram_tensor("x1_scratch", (S, D), F32, kind="Internal").ap()

    ctx = ExitStack()
    with ctx:
        def sb(name, shape, dt=F32, at=None):
            return (at or ctx).enter_context(nc.sbuf_tensor(name, shape, dt))

        def pair(name, shape, at=None):
            return sb(name + "_hi", shape, F32R, at), sb(name + "_lo", shape, F32R, at)

        bank = [ctx.enter_context(nc.psum_tensor(f"bank{b}", [P, 512], F32)) for b in range(NPSUM)]

        def sem(name):
            return ctx.enter_context(nc.semaphore(name))

        stage = [sb(f"stage{b}", [P, FLAT]) for b in range(2)]
        wsplit = [pair(f"w{b}", [P, FLAT]) for b in range(2)]
        rows = sb("rows", [P, 2, T, 512])
        bias_row = sb("ada_bias_row", [1, 2, CW])
        acc = sb("ada_acc", [P, 2, CW])
        gate_bc = sb("gate_bc", [P, D])
        ident = sb("ident", [P, P])
        small = sb("small_bf16", [P, 640], BF16)
        identb, causal = small[:, 0:128], small[:, 128:256]
        mask_q, mask_k = small[:, 256:384], small[:, 384:640]
        ones = sb("ones", [P, P])
        rope_sb = sb("rope_cs", [P, T, 2 * S_HD])
        cols_in = sb("columns", [P, 45])
        ccol_in = cols_in[:, 0:KD]
        ng = cols_in[:, KD:3 * KD].rearrange("p (l k) -> p l k", l=2)
        cw = cols_in[:, 24:40].rearrange("p (t w) -> p w t", w=4)
        ccol = sb("c_silu", [P, KD])
        amp = sb("amp", [P, 2, KD])
        shift = sb("shift", [P, 2, KD])
        latg = sb("latent_g_col", [P, 6])
        ssq = sb("sum_squares", [P, 2 * T])
        rstd = sb("rstd", [P, 2 * T])
        nt = sb("newton", [P, 4, 32])
        junk = sb("junk", [P, 2, P], BF16)
        work = sb("work", [P, 2, 512])
        tmp, dtmp = work[:, 0, :], work[:, 1, :]
        qrow = work[:, :, :].rearrange("p a (t d) -> p (a t) d", d=P)
        even = ExitStack()
        hT = pair("hT", [P, KD, S], even)
        negM = sb("m_neg_max_row", [M_HEADS, S], F32, even)
        hg = sb("head_g_bc", [P, M_HEADS * M_DV], F32, even)
        gate_b_col = sb("gate_bias_col", [M_HEADS, 2], F32, even)
        sink_bc = sb("sink_bc", [P, S_QH], F32, even)
        ifn = sb("gate_rows", [P, T, 2 * M_HEADS], F32, even)
        gcol = sb("m_g_col", [P, T, M_HEADS], F32, even)
        margs = sb("m_exponents", [P, 4, T, M_HEADS], F32, even)
        mden = sb("m_den", [P, T, M_HEADS], F32, even)
        hss = sb("m_sum_squares", [P, T, M_HEADS], F32, even)
        msc_t = sb("m_scale", [P, T, M_HEADS], F32, even)
        norm_mem = ExitStack()
        xhat = sb("xhat", [P, T, D], F32, norm_mem)
        norm_mem.close()
        win = ExitStack()
        vs = sb("s_v", [P, T, 2, 2, 64], F32R, win)
        ksT = pair("s_kT", [P, S], win)
        qsT = pair("s_qT", [P, S_G, P], win)
        sp = sb("s_probs", [P, 2, 2, 256], F32, win)
        spT = [pair(f"s_pT{b}", [P, 2, 2, P], win) for b in range(2)]
        sst = sb("s_stats", [P, 6, 12], F32, win)
        win.close()
        mem = ExitStack()
        raw = sb("m_raw", [P, S + 3], F32, mem)
        cacc = sb("m_conv", [P, S], F32, mem)
        qmT = pair("m_qT", [P, S], mem)
        kmT = pair("m_kT", [P, S], mem)
        vm = [pair(f"m_v{b}", [P, 2, VW], mem) for b in range(2)]
        Wt = sb("m_W", [P, 2, P], F32, mem)
        sw = pair("m_S", [P, 2, P], mem)
        kw = pair("m_kw", [P, P], mem)
        Cst = sb("m_C", [P, VW], F32, mem)
        Csp = [pair(f"m_Cs{b}", [P, VW], mem) for b in range(2)]
        mem.close()
        even.close()
        fin_mem = ExitStack()
        sb("place_of_hT_a", [P, 2, KD, S], F32, fin_mem)
        final_bc = sb("final_g_bc", [P, D], F32, fin_mem)
        fin_mem.close()
        lat = ExitStack()
        sb("place_of_hT_b", [P, 2, KD, S], F32, lat)
        craw = sb("c_rows", [P, T, CRW], F32, lat)
        lat.close()
        late = ExitStack()
        cT = pair("c_T", [P, 6, S], late)
        qrT = pair("c_qrT", [P, S], late)
        qmain = pair("c_qT", [P, S], late)
        kT = pair("c_kT", [P, S], late)
        vT = sb("c_v", [P, T, 2, P], F32R, late)
        osum = sb("c_out_sum", [P, P], F32, late)
        cp = sb("c_probs", [P, 2, S], F32, late)
        cpT = [pair(f"c_pT{b}", [P, 4, P], late) for b in range(CPT)]
        cst = sb("c_stats", [P, 6, 8], F32, late)
        late.close()

        filled = sem("psum_filled")
        vector_done = {}
        scalar_done = {}
        for s_ in order:
            k = s_[0]
            if k in DVE_KINDS and k not in vector_done:
                vector_done[k] = sem("vector_done_" + k)
            if k in ACT_KINDS and k not in scalar_done:
                scalar_done[k] = sem("scalar_done_" + k)
        split_done = sem("weight_chunks_split")
        v_split = sem("mlstm_v_split")
        dve_step = sem("vector_step")
        act_step = sem("scalar_step")
        const_in = sem("constants_in")
        even_in = sem("even_constants_in")
        final_in = sem("final_g_in")
        stage_in = [sem(f"stage{b}_in") for b in range(2)]
        x_in = [sem(f"x{i}_in") for i in range(T)]
        x_out = [sem(f"x1_{i}_out") for i in range(T)]
        qrot_out = [sem(f"q_rot_out{b}") for b in range(2)]
        qrot_in = sem("q_rot_in")
        y_out = sem("y_out")

        hx_tmp = [tmp, dtmp]
        tmp2 = tmp

        def bank_of(*step, m=0):
            return bank[bank_no[job[step] + m]]

        def grow(n):
            return rows[0:M_HEADS, 0, 2 * n:2 * n + 2, :].rearrange("p t d -> p (t d)")

        kn = rows[:, 0, 6:8, :].rearrange("p t d -> p (t d)").rearrange("p (t d) -> p t d", d=P)

        def split_dst(step):
            k, r = step[0], step[1:]
            cols = lambda half: slice(512 * half, 512 * half + 512)
            if k == "kTE":
                return [a[:, cols(r[0])] for a in ksT]
            if k == "aqTE":
                return [a[:, 2 * r[1]:2 * r[1] + 2, :].rearrange("p a q -> p (a q)") for a in qsT]
            if k == "apTE":
                return [a[:, :, 0:2, :] if r[0] else a[:, :, 1:2, :] for a in spT[nth[step] % 2]]
            if k == "yTE":
                return [a[:, r[1], cols(r[2])] for a in hT]
            if k == "cTE":
                return [a[:, r[0], cols(r[1])] for a in cT]
            if k == "qrTE":
                return [a[:, cols(r[1])] for a in qrT]
            if k == "pqTE":
                return [a[:, cols(r[1])] for a in qmain]
            if k == "pkTE":
                return [a[:, cols(r[1])] for a in kT]
            if k == "pvE":
                return [vT[:, 4 * r[1]:4 * r[1] + 4, m, :] for m in range(2)]
            n = min(4, r[1] + 1 - 4 * r[2])
            return [a[:, 0:n, :].rearrange("p t d -> p (t d)") for a in cpT[nth[step] % CPT]]

        def shaped(b, step):
            if step[0] == "apTE":
                v = b[:, :].rearrange("p (j k q) -> p j k q", j=2, k=2)
                return v if step[1] else v[:, :, 1:2, :]
            if step[0] == "mpTE":
                return b[:, 0:P * min(4, step[2] + 1 - 4 * step[3])]
            if step[0] == "aqTE":
                return b[:, 0:2 * P]
            if step[0] == "pvE":
                return b[:, :].rearrange("p (t d) -> p t d", d=P)
            return b[:, :]

        CONSTS = 16 * 3
        EVEN_CONSTS = 16 * 4
        block = ctx.enter_context(nc.Block())

        @block.sync
        def _(sp_eng):
            def const(dst, src, s_):
                sp_eng.dma_start(dst, src).then_inc(s_, 16)

            for step in order:
                k = step[0]
                if k == "xl":
                    l, i = step[1:]
                    if l == 2:
                        sp_eng.wait_ge(filled, filled_at["yT", 0, KD - 1, i // 4])
                    if l == 3:
                        sp_eng.wait_ge(filled, filled_at["yT", 1, KD - 1, i // 4])
                        sp_eng.wait_ge(x_out[i], 16)
                    src = x1_dram if l == 3 else x
                    sp_eng.dma_start(rows[:, :, i, :], src[i * P:(i + 1) * P, :].rearrange("p (a d) -> p a d", a=2))\
                        .then_inc(x_in[i], 16)
                elif step == ("cl", 0):
                    const(cols_in[:, :], columns, const_in)
                    const(gate_bc[:, 0:640], small_in, const_in)
                    const(ident[:, :], ident_in, const_in)
                elif step == ("cl", 1):
                    const(rope_sb[:, :, :], rope.rearrange("(t p) c -> p t c", p=P), even_in)
                    const(hg[:, :], head_g.rearrange("a d -> (a d)").partition_broadcast(P), even_in)
                    const(sink_bc[:, :], sinks.rearrange("a d -> (a d)").partition_broadcast(P), even_in)
                    const(gate_b_col[:, :], gate_b, even_in)
                elif k == "wl":
                    n = step[1]
                    what = stages[n]
                    if n >= 2:
                        before = stages[n - 2]
                        if before[0] == "ws":
                            sp_eng.wait_ge(split_done, before[1] + 1)
                        else:
                            sp_eng.wait_ge(vector_done["adaP"], nth["adaP", before[1], before[2], 3] + 1)
                    buf = stage[n % 2]
                    if what[0] == "adaA":
                        _, l, cc = what
                        sp_eng.dma_start(buf[:, 0:KD * CW].rearrange("p (k w) -> p k w", k=KD),
                                         ada_w[l].rearrange("(k p) n -> p k n", p=P)[:, :, CW * cc:CW * (cc + 1)])\
                            .then_inc(stage_in[n % 2], 16)
                        sp_eng.dma_start(bias_row[:, n % 2, :], ada_b[l:l + 1, CW * cc:CW * (cc + 1)])\
                            .then_inc(stage_in[n % 2], 16)
                    else:
                        for off, kt, width, pieces in CHUNKS[chunk_names[what[1]]]:
                            view = buf[:, off:off + kt * width].rearrange("p (k w) -> p k w", k=kt)
                            for name, col, w, to in pieces:
                                src = mat[name][0].rearrange("(k p) n -> p k n", p=P)
                                sp_eng.dma_start(view[:, :, to:to + w], src[:, :, col:col + w])\
                                    .then_inc(stage_in[n % 2], 16)
                elif k == "xs":
                    i = step[1]
                    sp_eng.wait_ge(vector_done["poE"], nth["poE", 0, 3, i] + 1)
                    sp_eng.dma_start(x1_dram[i * P:(i + 1) * P, :].rearrange("p (a d) -> p a d", a=2),
                                     rows[:, :, i, :]).then_inc(x_out[i], 16)
                elif k == "qs":
                    i = step[1]
                    sp_eng.wait_ge(vector_done["pqE"], nth["pqE", i] + 1)
                    sp_eng.dma_start(qr_dram[i * P:(i + 1) * P, :], cp[:, i % 2, 0:512]).then_inc(qrot_out[i % 2], 16)
                elif k == "ql":
                    a = step[1]
                    if a == 0:
                        for b in range(2):
                            sp_eng.wait_ge(qrot_out[b], 16 * T // 2)
                    else:
                        sp_eng.wait_ge(filled, filled_at["qrT", a - 1, 1])
                    sp_eng.dma_start(qrow[:, :, :], qr_dram.rearrange("(t p) c -> p t c", p=P)[:, :, P * a:P * (a + 1)])\
                        .then_inc(qrot_in, 16)
                elif k == "fin":
                    i = step[2]
                    sp_eng.wait_ge(vector_done[k], nth[step] + 1)
                    sp_eng.dma_start(out[0, i * P:(i + 1) * P, :], xhat[:, i, :]).then_inc(y_out, 16)
                elif k == "fg":
                    sp_eng.wait_ge(filled, filled_at["yT", 1, 0, 0])
                    sp_eng.dma_start(final_bc[:, :], final_g.partition_broadcast(P)).then_inc(final_in, 16)
            sp_eng.wait_ge(y_out, 16 * T)

        @block.gpsimd
        def _(pool):
            for step in order:
                if step[0] == "ws":
                    n = step[1]
                    size = max(b[0] + b[1] * b[2] for b in CHUNKS[chunk_names[n]])
                    pool.wait_ge(scalar_done[step[0]], nth[step] + 1)
                    nc.gpsimd.tensor_tensor(wsplit[n % 2][1][:, 0:size], stage[stage_no[step] % 2][:, 0:size],
                                            wsplit[n % 2][0][:, 0:size].bitcast(F32), ALU.subtract)\
                        .then_inc(split_done, 1)
                elif step[0] == "vsp":
                    _, p, i = step
                    pool.wait_ge(scalar_done[step[0]], nth[step] + 1)
                    nc.gpsimd.tensor_tensor(vm[i % 2][1][:, :, 0:M_DV],
                                            rows[:, 0, i, CW * p:CW * (p + 1)].rearrange("p (h d) -> p h d", h=2),
                                            vm[i % 2][0][:, :, 0:M_DV].bitcast(F32), ALU.subtract)\
                        .then_inc(v_split, 1)

        @block.tensor
        def _(pe):
            def start(step, m=0):
                n = job[step] + m
                if before_in_bank[n] is not None:
                    free, who = freeing(jobs[before_in_bank[n]])
                    if who == "dve":
                        pe.wait_ge(vector_done[free[0]], nth[free] + 1)
                    else:
                        pe.wait_ge(scalar_done[free[0]], nth[free] + 1)
                return bank[bank_no[n]]

            def mm3(o, a, b, at, bt, first, last, **kw):
                pe.matmul(o, a[0][at], b[0][bt], start=first, stop=False, **kw)
                pe.matmul(o, a[0][at], b[1][bt], start=False, stop=False, **kw)
                return pe.matmul(o, a[1][at], b[0][bt], start=False, stop=last, **kw)

            def mm_wide(wide, narrow, a, at, both, hi, first, last):
                pe.matmul(wide, a[0][at], both, start=first, stop=last, skip_group_check=True)
                return pe.matmul(narrow, a[1][at], hi, start=False, stop=last, skip_group_check=True)

            def weights(name):
                pe.wait_ge(split_done, chunk_no[name] + 1)
                return wsplit[chunk_no[name] % 2]

            def project(step, name, i, width):
                o = start(step)
                w = weights(name)
                for k in range(KD):
                    last = mm3(o[:, 0:width], hT, w, (slice(None), k, slice(i * P, (i + 1) * P)),
                               (slice(None), slice(k * width, (k + 1) * width)), k == 0, k == KD - 1)
                last.then_inc(filled, 1)

            def turn4(step, srcs, n=4):
                o = start(step)
                for j, src in enumerate(srcs):
                    if src is not None:
                        last = pe.transpose(o[:, j * P:(j + 1) * P], src, ident[:, :])
                last.then_inc(filled, 1)

            pe.wait_ge(const_in, CONSTS)
            pe.wait_ge(vector_done["ones"], nth["ones",] + 1)
            for step in order:
                k, r = step[0], step[1:]
                if k == "adaM":
                    l, cc = r
                    o = start(step)
                    pe.wait_ge(vector_done["adaP"], nth["adaP", l, cc, 3] + 1)
                    a = acc[:, nth[step] % 2, :]
                    if cc < 8:
                        for j in range(2):
                            last = pe.matmul(o[:, j:j + 1], a[:, j * P:(j + 1) * P], ones[:, 0:1], start=True, stop=True)
                    else:
                        last = pe.matmul(o[:, 0:CW], ones[:, :], a, start=True, stop=True)
                    last.then_inc(filled, 1)
                elif k == "xT":
                    l, kk, half = r
                    pe.wait_ge(vector_done["xh"], nth["xh", l, 4 * half + 3] + 1)
                    turn4(step, [xhat[:, i, kk * P:(kk + 1) * P] for i in range(4 * half, 4 * half + 4)])
                elif k == "kvg":
                    pe.wait_ge(vector_done["hx"], nth["hx", 0, KD - 1, r[0] // 4] + 1)
                    project(step, "kvg", r[0], 264)
                elif k == "sq":
                    project(step, ("sq", r[0]), r[1], CW)
                elif k == "gT":
                    half = r[0]
                    pe.wait_ge(scalar_done["kvgE"], nth["kvgE", 4 * half + 3] + 1)
                    for m in range(2):
                        o = start(step, m)
                        for ii in range(4):
                            last = pe.transpose(o[0:M_HEADS, ii * P:(ii + 1) * P],
                                                ifn[:, 4 * half + ii, M_HEADS * m:M_HEADS * (m + 1)], ident[:, :])
                        last.then_inc(filled, 1)
                elif k == "kT":
                    pe.wait_ge(vector_done["kvgE"], nth["kvgE", 4 * r[0] + 3] + 1)
                    turn4(step, [kn[:, i, :] for i in range(4 * r[0], 4 * r[0] + 4)])
                elif k == "aqT":
                    pe.wait_ge(vector_done["sqE"], nth["sqE", 1, r[0]] + 1)
                    turn4(step, [rows[:, 1, r[0], j * P:(j + 1) * P] for j in (2 * r[1], 2 * r[1] + 1)])
                elif k == "asc":
                    i, g, ap = r
                    pe.wait_ge(vector_done["aqTE"], nth["aqTE", i, ap] + 1)
                    pe.wait_ge(vector_done["kTE"], nth["kTE", 1 if i > 3 else 0] + 1)
                    o = start(step)
                    part = slice(64 * g, 64 * g + 64)
                    lo_key, at = ((i - 1) * P, 0) if i else (0, P)
                    for j in range(2):
                        dst = o[:, 256 * j + at:256 * j + 256]
                        mm3(dst, qsT, ksT, (part, 2 * ap + j, slice(None)), (part, slice(lo_key, (i + 1) * P)), True, False)
                        last = pe.matmul(dst, mask_q[part, :], mask_k[part, at:256], start=False, stop=True)
                    last.then_inc(filled, 1)
                elif k == "apT":
                    i, g, ap = r
                    pe.wait_ge(scalar_done["aex"], nth["aex", i, g, ap] + 1)
                    u = nth["aex", i, g, ap] % 2
                    turn4(step, [sp[:, u, j // 2, (j % 2) * P:(j % 2 + 1) * P] if i or j % 2 else None for j in range(4)])
                elif k == "apv":
                    i, g, ap = r
                    pe.wait_ge(vector_done["apTE"], nth["apTE", i, g, ap] + 1)
                    pe.wait_ge(vector_done["kvgE"], nth["kvgE", i] + 1)
                    o = start(step)
                    u = nth["apTE", i, g, ap] % 2
                    kts = (0, 1) if i else (1,)
                    for j in range(2):
                        for kt in kts:
                            v = vs[:, i - 1 + kt, g, :, :]
                            last = mm_wide(o[:, P * j:P * j + P], o[:, P * j:P * j + 64], spT[u],
                                           (slice(None), j, kt, slice(None)), v.rearrange("p m d -> p (m d)"), v[:, 0, :],
                                           kt == kts[0], kt == 1)
                    last.then_inc(filled, 1)
                elif k == "colsT":
                    pe.wait_ge(vector_done["rows"], nth["rows",] + 1)
                    o = start(step)
                    for q, src in enumerate((grow(0), negM[:, :], grow(2))):
                        for i in range(T):
                            pe.transpose(o[:, 32 * q + 4 * i:32 * q + 4 * i + 4], src[:, i * P:(i + 1) * P],
                                         ident[0:M_HEADS, 0:M_HEADS])
                    for q, src in enumerate((grow(2), negM[:, :])):
                        for h in range(M_HEADS):
                            at = 96 + 32 * q + 8 * h
                            last = pe.matmul(o[:, at:at + T], ident[0:M_HEADS, h:h + 1].broadcast_to([M_HEADS, P]),
                                             src.rearrange("h (t s) -> h t s", s=P)[:, :, P - 1], start=True, stop=True)
                    last.then_inc(filled, 1)
                elif k == "mqk":
                    p, which, half = r
                    o = start(step)
                    w = weights(("mqk", p))
                    for kk in range(KD):
                        last = mm3(o[:, :], w, hT, (slice(None), slice(kk * CW + P * which, kk * CW + P * which + P)),
                                   (slice(None), kk, slice(512 * half, 512 * half + 512)), kk == 0, kk == KD - 1)
                    last.then_inc(filled, 1)
                elif k == "mv":
                    project(step, ("mv", r[0]), r[1], CW)
                elif k == "mB":
                    p, i = r
                    o = start(step)
                    if p == 0 and i == 0:
                        pe.wait_ge(vector_done["rows"], nth["rows",] + 1)
                    for j in range(2):
                        h = 2 * p + j
                        dst = o[:, j * P:(j + 1) * P]
                        pe.matmul(dst, ident[0:M_HEADS, h:h + 1].broadcast_to([M_HEADS, P]),
                                  negM[:, i * P:(i + 1) * P], start=True, stop=False)
                        last = pe.matmul(dst, identb, causal, start=False, stop=True)
                    last.then_inc(filled, 1)
                elif k == "mS":
                    p, i = r
                    pe.wait_ge(vector_done["conv"], nth["conv", p, 1] + 1)
                    pe.wait_ge(vector_done["qksp"], nth["qksp", p, 1] + 1)
                    for j in range(2):
                        o = start(step, j)
                        at = (slice(64 * j, 64 * j + 64), slice(i * P, (i + 1) * P))
                        mm3(o[:, 0:P], kmT, qmT, at, at, True, True).then_inc(filled, 1)
                elif k == "kN":
                    p, i = r
                    turn4(step, [cacc[:, i * P:(i + 1) * P]])
                elif k == "mO":
                    p, i = r
                    pe.wait_ge(vector_done["mSE"], nth["mSE", p, i] + 1)
                    pe.wait_ge(v_split, T * p + i + 1)
                    for j in range(2):
                        o = start(step, j)
                        last = mm3(o[:, 0:VW], sw, vm[i % 2], (slice(None), j, slice(None)), (slice(None), j, slice(None)),
                                   True, True)
                        if i:
                            pe.wait_ge(vector_done["mCE"], nth["mCE", p, i - 1] + 1)
                            part = slice(64 * j, 64 * j + 64)
                            last = mm3(o[:, 256:256 + VW], qmT, Csp[(i - 1) % 2], (part, slice(i * P, (i + 1) * P)),
                                       (part, slice(None)), True, True)
                        last.then_inc(filled, 1)
                elif k == "mC":
                    p, i = r
                    pe.wait_ge(vector_done["kNE"], nth["kNE", p, i] + 1)
                    pe.wait_ge(v_split, T * p + i + 1)
                    o = start(step)
                    for j in range(2):
                        last = mm3(o[:, 256 * j:256 * j + VW], kw, vm[i % 2], (slice(None), slice(None)),
                                   (slice(None), j, slice(None)), True, True)
                    last.then_inc(filled, 1)
                elif k == "mo":
                    project(step, ("mo", r[0]), r[1], CW)
                elif k == "z":
                    project(step, ("z", r[0], r[1]), r[2], CW)
                elif k == "yT":
                    l, kk, half = r
                    if l == 0:
                        pe.wait_ge(vector_done["zE"], nth["zE", 0, kk // 2, 4 * half + 3] + 1)
                    else:
                        pe.wait_ge(vector_done["mno"], nth["mno", C_HEADS - 1, T - 1] + 1)
                    turn4(step, [rows[:, kk // 4, i, (kk % 4) * P:(kk % 4 + 1) * P] for i in range(4 * half, 4 * half + 4)])
                elif k == "po":
                    l, oc, i = r
                    pe.wait_ge(vector_done["yTE"], nth["yTE", l, KD - 1, i // 4] + 1)
                    project(step, ("out", l, oc), i, CW)
                elif k == "lat":
                    cc, i = r
                    pe.wait_ge(vector_done["hx"], nth["hx", 1, KD - 1, i // 4] + 1)
                    project(step, ("lat", cc), i, LAT_W[cc])
                elif k == "cT":
                    kk, half = r
                    pe.wait_ge(vector_done["lsc"], nth["lsc", 4 * half + 3] + 1)
                    turn4(step, [craw[:, i, kk * P:(kk + 1) * P] for i in range(4 * half, 4 * half + 4)])
                elif k == "pq":
                    i = r[0]
                    pe.wait_ge(vector_done["cTE"], nth["cTE", KQ - 1, i // 4] + 1)
                    o = start(step)
                    w = weights("uqr")
                    for kk in range(KQ):
                        last = mm3(o[:, :], cT, w, (slice(None), kk, slice(i * P, (i + 1) * P)),
                                   (slice(None), slice(kk * 512, (kk + 1) * 512)), kk == 0, kk == KQ - 1)
                    last.then_inc(filled, 1)
                elif k == "qrT":
                    a, half = r
                    pe.wait_ge(qrot_in, 16 * (a + 1))
                    turn4(step, [qrow[:, i, :] for i in range(4 * half, 4 * half + 4)])
                elif k in ("pqT", "pkT"):
                    h, half = r
                    o = start(step)
                    w = weights(("hp", h // 2))
                    pe.wait_ge(vector_done["cTE"], nth["cTE", 5, 1] + 1)
                    j, kts = h % 2, KQ if k == "pqT" else KKV
                    for kk in range(kts):
                        at = kk * 256 + P * j if k == "pqT" else 768 + kk * 512 + 256 * j
                        row = kk if k == "pqT" else KQ + kk
                        last = mm3(o[:, :], w, cT, (slice(None), slice(at, at + P)),
                                   (slice(None), row, slice(512 * half, 512 * half + 512)), kk == 0, kk == kts - 1)
                    last.then_inc(filled, 1)
                elif k == "pv":
                    h, half = r
                    o = start(step)
                    w = weights(("hp", h // 2))
                    for ii in range(4):
                        i = 4 * half + ii
                        for kk in range(KKV):
                            at = 768 + kk * 512 + 256 * (h % 2) + P
                            last = mm3(o[:, ii * P:(ii + 1) * P], cT, w, (slice(None), KQ + kk, slice(i * P, (i + 1) * P)),
                                       (slice(None), slice(at, at + P)), kk == 0, kk == KKV - 1)
                    last.then_inc(filled, 1)
                elif k == "msc":
                    h, i, b = r
                    pe.wait_ge(vector_done["pqTE"], nth["pqTE", h, i // 4] + 1)
                    pe.wait_ge(vector_done["pkTE"], nth["pkTE", h, i // 4] + 1)
                    pe.wait_ge(vector_done["qrTE"], nth["qrTE", h // 2, i // 4] + 1)
                    o = start(step)
                    nk = min(512, P * (i + 1) - 512 * b)
                    part = slice(64 * (h % 2), 64 * (h % 2) + 64)
                    keys, tile = slice(512 * b, 512 * b + nk), slice(i * P, (i + 1) * P)
                    mm3(o[:, 0:nk], qmain, kT, (slice(None), tile), (slice(None), keys), True, False)
                    diagonal = 512 * b + nk == P * (i + 1)
                    if diagonal:
                        pe.matmul(o[:, nk - P:nk], mask_q[part, :], mask_k[part, P:256], start=False, stop=False,
                                  skip_group_check=True)
                    last = mm3(o[:, 0:nk], qrT, cT, (part, tile), (part, 5, keys), False, True)
                    last.then_inc(filled, 1)
                elif k == "mpT":
                    h, i, b = r
                    pe.wait_ge(scalar_done["mex"], nth["mex", h, i] + 1)
                    u = nth["mex", h, i] % 2
                    n = min(4, i + 1 - 4 * b)
                    turn4(step, [cp[:, u, (4 * b + j) * P:(4 * b + j + 1) * P] for j in range(n)])
                elif k == "mpv":
                    h, i, b = r
                    pe.wait_ge(vector_done["mpTE"], nth["mpTE", h, i, b] + 1)
                    pe.wait_ge(vector_done["pvE"], nth["pvE", h, i // 4] + 1)
                    o = start(step) if b == 0 else bank[bank_no[job[step]]]
                    src = cpT[nth["mpTE", h, i, b] % CPT]
                    for j in range(min(4, i + 1 - 4 * b)):
                        kt = 4 * b + j
                        last = mm_wide(o[:, 0:2 * P], o[:, 0:P], src, (slice(None), j, slice(None)),
                                       vT[:, kt, :, :].rearrange("p m d -> p (m d)"), vT[:, kt, 0, :], kt == 0, kt == i)
                    if b == i // 4:
                        last.then_inc(filled, 1)

        @block.scalar
        def _(act):
            steps_done = [0]

            def again(ins):
                steps_done[0] += 1
                ins.then_inc(act_step, 1)
                act.wait_ge(act_step, steps_done[0])

            act.wait_ge(const_in, CONSTS)
            before = None
            for step in order:
                k, r = step[0], step[1:]
                if k not in ACT_KINDS:
                    continue
                if before:
                    act.wait_ge(scalar_done[before[0]], nth[before] + 1)
                before = step
                done = scalar_done[k]
                if k == "csilu":
                    nc.scalar.activation(ccol[:, :], ccol_in, ACT.Silu).then_inc(done, 1)
                elif k == "ws":
                    n = r[0]
                    s_no = stage_no[step]
                    size = max(b[0] + b[1] * b[2] for b in CHUNKS[chunk_names[n]])
                    act.wait_ge(stage_in[s_no % 2], stage_value[s_no])
                    if n >= 2:
                        act.wait_ge(filled, last_job[chunk_names[n - 2]])
                    nc.scalar.activation(wsplit[n % 2][0][:, 0:size], stage[s_no % 2][:, 0:size], ACT.Copy)\
                        .then_inc(done, 1)
                elif k == "xsq":
                    l, i = r
                    if l == 0:
                        act.wait_ge(x_in[i], 16)
                    else:
                        act.wait_ge(vector_done["poE"], nth["poE", l - 1, 3, i] + 1)
                    nc.scalar.activation(xhat[:, i, :].rearrange("p (a d) -> p a d", a=2), rows[:, :, i, :], ACT.Square,
                                         accum_out=ssq[:, i:i + 1]).then_inc(done, 1)
                elif k == "hx":
                    l, kk, half = r
                    act.wait_ge(filled, filled_at["xT", l, kk, half])
                    if kk == 0 and half == 0:
                        act.wait_ge(vector_done["adaE"], nth["adaE", l, 7] + 1)
                    if nth[step] >= 2:
                        act.wait_ge(vector_done["hx"], nth[step] - 1)
                    nc.scalar.activation(hx_tmp[nth[step] % 2][:, :],
                                         bank_of("xT", *r)[:, :], ACT.Identity,
                                         bias=shift[:, l, kk:kk + 1], scale=amp[:, l, kk:kk + 1]).then_inc(done, 1)
                elif k == "kvgE":
                    i = r[0]
                    act.wait_ge(filled, filled_at["kvg", i])
                    b = bank_of("kvg", i)
                    nc.scalar.activation(vs[:, i, :, 0, :], b[:, 128:256].rearrange("p (g d) -> p g d", g=2), ACT.Copy)
                    nc.scalar.activation(ifn[:, i, :], b[:, 256:264], ACT.Copy).then_inc(done, 1)
                elif k in ("kTE", "aqTE", "apTE", "yTE", "qrTE", "pqTE", "pkTE", "pvE", "mpTE", "cTE"):
                    src = (k[:-1], *r)
                    act.wait_ge(filled, filled_at[src])
                    b = bank_of(*src)
                    hi = split_dst(step)[0]
                    if k == "aqTE" and r[0]:
                        act.wait_ge(filled, filled_at["asc", r[0] - 1, 1, r[1]])
                    if k == "apTE" and nth[step] >= 2:
                        act.wait_ge(filled, filled_at["apv", *order_at[k, nth[step] - 2][1:]])
                    if k == "mpTE" and nth[step] >= CPT:
                        act.wait_ge(filled, filled_at["mpv", *order_at[k, nth[step] - CPT][1:]])
                    scale = latg[:, r[0]:r[0] + 1] if k == "cTE" else 1.0
                    if k == "cTE":
                        act.wait_ge(vector_done["ones"], nth["ones",] + 1)
                    nc.scalar.activation(hi, shaped(b, step), ACT.Copy, scale=scale).then_inc(done, 1)
                elif k == "rowsB":
                    act.wait_ge(vector_done["rowsA"], nth["rowsA",] + 1)
                    again(nc.scalar.activation(grow(2), grow(2), ACT.Exp))
                    nc.scalar.activation(grow(2), grow(2), ACT.Ln, bias=1.0).then_inc(done, 1)
                elif k == "aex":
                    i, g, ap = r
                    act.wait_ge(vector_done["asm"], nth["asm", *r] + 1)
                    act.wait_ge(filled, filled_at["asc", *r])
                    u = nth[step] % 2
                    st = sst[:, nth[step] % 6, :]
                    if nth[step] >= 2:
                        act.wait_ge(filled, filled_at["apT", *order_at[k, nth[step] - 2][1:]])
                    b = bank_of("asc", *r)
                    at = 0 if i else P
                    nc.scalar.activation(st[:, 4:6], st[:, 4:6], ACT.Exp)
                    for j in range(2):
                        last = nc.scalar.activation(sp[:, u, j, at:256], b[:, 256 * j + at:256 * j + 256], ACT.Exp,
                                                    bias=st[:, 2 + j:3 + j], scale=S_SCALE,
                                                    accum_out=st[:, 6 + j:7 + j])
                    last.then_inc(done, 1)
                elif k == "cols":
                    act.wait_ge(vector_done["colsE"], nth["colsE",] + 1)
                    nc.scalar.activation(margs[:, :, :, :], margs[:, :, :, :], ACT.Exp).then_inc(done, 1)
                elif k == "mqkE":
                    p, which, half = r
                    act.wait_ge(filled, filled_at["mqk", *r])
                    if which or p:
                        act.wait_ge(vector_done["conv"], nth["conv", p if which else p - 1, 0 if which else 1] + 1)
                    else:
                        act.wait_ge(vector_done["cols"], nth["cols",] + 1)
                    nc.scalar.activation(raw[:, 3 + 512 * half:3 + 512 * half + 512], bank_of("mqk", *r)[:, :],
                                         ACT.Copy).then_inc(done, 1)
                elif k == "silu":
                    p, which = r
                    act.wait_ge(vector_done["conv"], nth["conv", p, which] + 1)
                    again(nc.scalar.activation(cacc[:, :], cacc[:, :], ACT.Silu))
                    nc.scalar.activation((kmT if which else qmT)[0][:, :], cacc[:, :], ACT.Copy,
                                         scale=M_SCALE if which else 1.0).then_inc(done, 1)
                elif k == "mvE":
                    p, i = r
                    act.wait_ge(filled, filled_at["mv", p, i])
                    nc.scalar.activation(rows[:, 0, i, CW * p:CW * (p + 1)], bank_of("mv", p, i)[:, 0:CW], ACT.Copy)\
                        .then_inc(done, 1)
                elif k == "vsp":
                    p, i = r
                    if p or i >= 2:
                        b = ("vsp", p, i - 2) if i >= 2 else ("vsp", p - 1, i + T - 2)
                        act.wait_ge(filled, filled_at["mO", *b[1:]])
                    else:
                        act.wait_ge(vector_done["cols"], nth["cols",] + 1)
                    act.wait_ge(scalar_done["mvE"], nth["mvE", p, i] + 1)
                    nc.scalar.activation(vm[i % 2][0][:, :, 0:M_DV],
                                         rows[:, 0, i, CW * p:CW * (p + 1)].rearrange("p (h d) -> p h d", h=2),
                                         ACT.Copy).then_inc(done, 1)
                elif k == "mBE":
                    p, i = r
                    act.wait_ge(filled, filled_at["mB", p, i])
                    if nth[step] >= 1:
                        act.wait_ge(vector_done["mSE"], nth[step])
                    for j in range(2):
                        last = nc.scalar.activation(Wt[:, j, :], bank_of("mB", p, i)[:, j * P:(j + 1) * P],
                                                    ACT.Exp, bias=gcol[:, i, 2 * p + j:2 * p + j + 1])
                    last.then_inc(done, 1)
                elif k == "hsq":
                    p, i = r
                    act.wait_ge(vector_done["mOE"], nth["mOE", p, i] + 1)
                    for j in range(2):
                        h = 2 * p + j
                        last = nc.scalar.activation(junk[:, j, :], rows[:, 0, i, M_DV * h:M_DV * (h + 1)], ACT.Square,
                                                    accum_out=hss[:, i, h:h + 1])
                    last.then_inc(done, 1)
                elif k in ("moE", "zE"):
                    src = (k[:-1], *r)
                    act.wait_ge(filled, filled_at[src])
                    b = bank_of(*src)
                    i = r[-1]
                    if k == "zE" and r[0] == 1:
                        zc = r[1]
                        act.wait_ge(x_out[i], 16)
                        act.wait_ge(vector_done["xh"], nth["xh", 1, i] + 1)
                        nc.scalar.activation(rows[:, zc // 2, i, CW * (zc % 2):CW * (zc % 2 + 1)], b[:, 0:CW], ACT.Silu)\
                            .then_inc(done, 1)
                    else:
                        par = gate_no[step] % 2
                        if gate_no[step] >= 2:
                            act.wait_ge(vector_done[gate_steps[gate_no[step] - 2][0]], nth[gate_steps[gate_no[step] - 2]] + 1)
                        nc.scalar.activation(tmp[:, CW * par:CW * (par + 1)], b[:, 0:CW],
                                             ACT.Tanh if k == "moE" else ACT.Silu,
                                             scale=0.5 if k == "moE" else 1.0).then_inc(done, 1)
                elif k == "latE":
                    cc, i = r
                    act.wait_ge(filled, filled_at["lat", cc, i])
                    nc.scalar.activation(craw[:, i, CW * cc:CW * cc + LAT_W[cc]], bank_of("lat", cc, i)[:, 0:LAT_W[cc]],
                                         ACT.Copy).then_inc(done, 1)
                elif k == "lsq":
                    i = r[0]
                    act.wait_ge(scalar_done["latE"], nth["latE", 2, i] + 1)
                    again(nc.scalar.activation(tmp[:, 0:C_QL], craw[:, i, 0:C_QL], ACT.Square, accum_out=ssq[:, i:i + 1]))
                    nc.scalar.activation(tmp[:, 0:C_KVL], craw[:, i, C_QL:C_QL + C_KVL], ACT.Square,
                                         accum_out=ssq[:, T + i:T + i + 1]).then_inc(done, 1)
                elif k == "mex":
                    h, i = r
                    act.wait_ge(vector_done["msm"], nth["msm", h, i] + 1)
                    u = nth[step] % 2
                    st = cst[:, nth[step] % 6, :]
                    if nth[step] >= 2:
                        b = order_at[k, nth[step] - 2]
                        act.wait_ge(filled, filled_at["mpT", b[1], b[2], b[2] // 4])
                    for b in range(i // 4 + 1):
                        nk = min(512, P * (i + 1) - 512 * b)
                        last = nc.scalar.activation(cp[:, u, 512 * b:512 * b + nk], bank_of("msc", h, i, b)[:, 0:nk],
                                                    ACT.Exp, bias=st[:, 2:3], scale=C_SCALE,
                                                    accum_out=st[:, 3 + b:4 + b])
                    last.then_inc(done, 1)

        @block.vector
        def _(dve):
            steps_done = [0]

            def again(ins):
                steps_done[0] += 1
                ins.then_inc(dve_step, 1)
                dve.wait_ge(dve_step, steps_done[0])

            V = nc.vector

            def rotate(dst, src, i, n, done=None):
                cos = rope_sb[:, i:i + 1, 0:64].broadcast_to([P, n, 64])
                a = dtmp[:, 0:64 * n].rearrange("p (n d) -> p n d", d=64)
                b = tmp2[:, 0:64 * n].rearrange("p (n d) -> p n d", d=64)
                V.tensor_tensor(a, src, cos, ALU.mult)
                for m in range(2):
                    sin = rope_sb[:, i:i + 1, 64 + 32 * m:96 + 32 * m].broadcast_to([P, n, 32])
                    last = V.tensor_tensor(b[:, :, 32 * m:32 * m + 32], src[:, :, 32 * (1 - m):32 * (1 - m) + 32], sin, ALU.mult)
                again(last)
                ins = V.tensor_tensor(dst, a, b, ALU.add)
                if done:
                    ins.then_inc(done, 1)
                return ins

            def inverse_root(dst, v, n, done):
                y, a = nt[:, 1, 0:n], nt[:, 2, 0:n]
                again(V.tensor_single_scalar(a.bitcast(I32), v.bitcast(I32), 1, ALU.arith_shift_right))
                again(V.tensor_scalar(y.bitcast(I32), a.bitcast(I32), -1.0, float(0x5F3759DF), ALU.mult, ALU.add))
                for it in range(3):
                    again(V.scalar_tensor_tensor(out=a, in0=y, scalar=-0.5, in1=y, op0=ALU.mult, op1=ALU.mult))
                    again(V.tensor_tensor(a, a, v, ALU.mult))
                    ins = V.scalar_tensor_tensor(out=y if it < 2 else dst, in0=a, scalar=1.5, in1=y,
                                                 op0=ALU.add, op1=ALU.mult)
                    if it < 2 or done is None:
                        again(ins)
                    else:
                        ins.then_inc(done, 1)

            dve.wait_ge(const_in, CONSTS)
            before = None
            for step in order:
                k, r = step[0], step[1:]
                if k not in DVE_KINDS or step[:2] == ("zE", 1):
                    continue
                if before:
                    dve.wait_ge(vector_done[before[0]], nth[before] + 1)
                before = step
                done = vector_done[k]
                if k == "ones":
                    V.tensor_copy(latg[:, 0:5], cols_in[:, 40:45])
                    V.memset(latg[:, 5:6], 1.0)
                    V.tensor_copy(small[:, :], gate_bc[:, 0:640])
                    V.memset(ones[:, :], 1.0).then_inc(done, 1)
                elif k == "adaA":
                    l, cc = r
                    if cc == 0 and l == 0:
                        dve.wait_ge(scalar_done["csilu"], nth["csilu",] + 1)
                    s_no = stage_no[step]
                    dve.wait_ge(stage_in[s_no % 2], stage_value[s_no])
                    par = nth[step] % 2
                    if nth[step] >= 2:
                        dve.wait_ge(filled, filled_at["adaM", *order_at["adaA", nth[step] - 2][1:]])
                    a = acc[:, par, :]
                    w = stage[s_no % 2][:, 0:KD * CW].rearrange("p (k w) -> p k w", k=KD)
                    again(V.tensor_scalar(a, w[:, 0, :], ccol[:, 0:1], None, ALU.mult))
                    V.scalar_tensor_tensor(out=a, in0=w[:, 1, :], scalar=ccol[:, 1:2], in1=a,
                                           op0=ALU.mult, op1=ALU.add).then_inc(done, 1)
                elif k == "adaP":
                    l, cc, q = r
                    s_no = stage_no["adaA", l, cc]
                    par = nth["adaA", l, cc] % 2
                    a = acc[:, par, :]
                    w = stage[s_no % 2][:, 0:KD * CW].rearrange("p (k w) -> p k w", k=KD)
                    for kk in range(2 * q, 2 * q + 2):
                        ins = V.scalar_tensor_tensor(out=a, in0=w[:, kk, :], scalar=ccol[:, kk:kk + 1], in1=a,
                                                     op0=ALU.mult, op1=ALU.add)
                        if kk % 2 == 0 or q == 3:
                            again(ins)
                    if q == 3:
                        ins = V.tensor_tensor(acc[0:1, par, :], acc[0:1, par, :], bias_row[:, s_no % 2, :], ALU.add)
                    ins.then_inc(done, 1)
                elif k == "adaE":
                    l, cc = r
                    dve.wait_ge(filled, filled_at["adaM", l, cc])
                    b = bank_of("adaM", l, cc)
                    if cc < 4:
                        ins = V.tensor_copy(shift[:, l, 2 * cc:2 * cc + 2], b[:, 0:2])
                    elif cc < 8:
                        at = slice(2 * cc - 8, 2 * cc - 6)
                        ins = V.scalar_tensor_tensor(out=amp[:, l, at], in0=b[:, 0:2], scalar=1.0, in1=ng[:, l, at],
                                                     op0=ALU.add, op1=ALU.mult)
                    else:
                        ins = V.tensor_copy(gate_bc[:, CW * (cc - 8):CW * (cc - 7)], b[:, 0:CW])
                    ins.then_inc(done, 1)
                elif k == "rs":
                    l, half = r
                    at = slice(4 * half, 4 * half + 4)
                    dve.wait_ge(scalar_done["xsq"], nth["xsq", l, 4 * half + 3] + 1)
                    again(V.tensor_scalar(nt[:, 0, 0:4], ssq[:, at], 1.0 / D, EPS, ALU.mult, ALU.add))
                    inverse_root(rstd[:, at], nt[:, 0, 0:4], 4, done)
                    dve.wait_ge(vector_done[k], nth[step] + 1)
                elif k == "xh":
                    l, i = r
                    V.tensor_scalar(xhat[:, i, :].rearrange("p (a d) -> p a d", a=2), rows[:, :, i, :],
                                    rstd[:, i:i + 1], None, ALU.mult).then_inc(done, 1)
                elif k == "hx":
                    l, kk, half = r
                    dve.wait_ge(scalar_done[k], nth[step] + 1)
                    src = hx_tmp[nth[step] % 2]
                    at = slice(512 * half, 512 * half + 512)
                    again(V.tensor_copy(hT[0][:, kk, at], src[:, :]))
                    V.tensor_tensor(hT[1][:, kk, at], src[:, :], hT[0][:, kk, at].bitcast(F32), ALU.subtract)\
                        .then_inc(done, 1)
                elif k == "kvgE":
                    i = r[0]
                    dve.wait_ge(scalar_done[k], nth[step] + 1)
                    if i == 0:
                        dve.wait_ge(even_in, EVEN_CONSTS)
                    b = bank_of("kvg", i)
                    rotate(kn[:, i, :].rearrange("p (n d) -> p n d", d=64), b[:, 0:P].rearrange("p (n d) -> p n d", d=64), i, 2)
                    V.tensor_tensor(vs[:, i, :, 1, :], b[:, 128:256].rearrange("p (g d) -> p g d", g=2),
                                    vs[:, i, :, 0, :].bitcast(F32), ALU.subtract)\
                        .then_inc(done, 1)
                elif k == "sqE":
                    g, i = r
                    dve.wait_ge(filled, filled_at["sq", g, i])
                    b = bank_of("sq", g, i)
                    dst = rows[:, 1, i, :].rearrange("p (a q d) -> p a q d", q=2, d=64)[:, :, g, :]
                    rotate(dst, b[:, 0:CW].rearrange("p (n d) -> p n d", d=64), i, 4, done)
                elif k == "pqE":
                    i = r[0]
                    dve.wait_ge(filled, filled_at["pq", i])
                    b = bank_of("pq", i)
                    if i >= 2:
                        dve.wait_ge(qrot_out[i % 2], 16 * (i // 2))
                    rotate(cp[:, i % 2, 0:512].rearrange("p (n d) -> p n d", d=64),
                           b[:, :].rearrange("p (n d) -> p n d", d=64), i, 8, done)
                elif k in ("kTE", "aqTE", "apTE", "yTE", "qrTE", "pqTE", "pkTE", "pvE", "mpTE", "cTE"):
                    dve.wait_ge(scalar_done[k], nth[step] + 1)
                    b = shaped(bank_of(k[:-1], *r), step)
                    hi, lo = split_dst(step)
                    if k == "cTE":
                        V.scalar_tensor_tensor(out=lo, in0=b, scalar=latg[:, r[0]:r[0] + 1], in1=hi.bitcast(F32),
                                               op0=ALU.mult, op1=ALU.subtract).then_inc(done, 1)
                    else:
                        V.tensor_tensor(lo, b, hi.bitcast(F32), ALU.subtract).then_inc(done, 1)
                elif k == "gTE":
                    half = r[0]
                    dve.wait_ge(filled, filled_at["gT", half])
                    for m in range(2):
                        ins = V.tensor_scalar(grow(m)[:, 512 * half:512 * half + 512],
                                              bank_of("gT", half, m=m)[0:M_HEADS, :], gate_b_col[:, m:m + 1], None, ALU.add)
                    ins.then_inc(done, 1)
                elif k == "rowsA":
                    dve.wait_ge(vector_done["gTE"], nth["gTE", 1] + 1)
                    V.scalar_tensor_tensor(out=grow(2), in0=grow(1), scalar=-1.0, in1=grow(1), op0=ALU.mult, op1=ALU.min)\
                        .then_inc(done, 1)
                    again(V.memset(negM[:, :], 1.0))
                    again(V.memset(negM[:, :].rearrange("h (t s) -> h t s", s=P)[:, :, 0:1], 0.0))
                elif k == "rows":
                    dve.wait_ge(scalar_done["rowsB"], nth["rowsB",] + 1)
                    i_row, f_row, b_row = grow(0), grow(1), grow(2)
                    again(V.scalar_tensor_tensor(out=f_row, in0=f_row, scalar=0.0, in1=b_row, op0=ALU.min, op1=ALU.subtract))
                    again(V.tensor_tensor_scan(b_row, negM[:, :], f_row, 0.0, ALU.mult, ALU.add))
                    again(V.tensor_tensor(i_row, i_row, b_row, ALU.subtract))
                    again(V.memset(negM[:, :], 0.0))
                    tiles = lambda a: a.rearrange("h (t s) -> h t s", s=P)
                    again(V.tensor_copy(tiles(negM[:, :])[:, 1:T, 0:1], tiles(b_row)[:, 0:T - 1, P - 1:P]))
                    again(V.tensor_tensor_scan(f_row, negM[:, :], i_row, 0.0, ALU.add, ALU.max))
                    again(V.tensor_tensor(b_row, b_row, f_row, ALU.add))
                    V.tensor_scalar(negM[:, :], f_row, -1.0, None, ALU.mult).then_inc(done, 1)
                elif k == "asm":
                    i, g, ap = r
                    dve.wait_ge(filled, filled_at["asc", *r])
                    at = 0 if i else P
                    st = sst[:, nth[step] % 6, :]
                    src = bank_of("asc", *r)[:, :].rearrange("p (j k) -> p j k", j=2)[:, :, at:256]
                    head = 4 * g + 2 * ap
                    again(V.tensor_reduce(st[:, 0:2], src, AX, ALU.max))
                    again(V.scalar_tensor_tensor(out=st[:, 0:2], in0=st[:, 0:2], scalar=S_SCALE, in1=sink_bc[:, head:head + 2],
                                                 op0=ALU.mult, op1=ALU.max))
                    V.tensor_scalar(st[:, 2:4], st[:, 0:2], -1.0, None, ALU.mult)
                    V.tensor_tensor(st[:, 4:6], sink_bc[:, head:head + 2], st[:, 0:2], ALU.subtract).then_inc(done, 1)
                elif k == "ano":
                    i, g, ap = r
                    st = sst[:, nth["asm", i, g, ap] % 6, :]
                    dve.wait_ge(scalar_done["aex"], nth["aex", *r] + 1)
                    again(V.tensor_tensor(st[:, 8:10], st[:, 4:6], st[:, 6:8], ALU.add))
                    again(V.reciprocal(st[:, 10:12], st[:, 8:10]))
                    dve.wait_ge(filled, filled_at["apv", *r])
                    col = 64 * (4 * g + 2 * ap)
                    b = bank_of("apv", *r)[:, 0:2 * P].rearrange("p (j m d) -> p j m d", j=2, m=2)
                    osum_ = dtmp[:, 0:P].rearrange("p (j d) -> p j d", j=2)
                    again(V.tensor_copy(osum_, b[:, :, 1, :]))
                    again(V.tensor_tensor(osum_, b[:, :, 0, :], osum_, ALU.add))
                    V.tensor_tensor(rows[:, 1, i, col:col + P].rearrange("p (j d) -> p j d", j=2), osum_,
                                    st[:, 10:12].unsqueeze(2).broadcast_to([P, 2, 64]), ALU.mult).then_inc(done, 1)
                elif k == "colsE":
                    dve.wait_ge(filled, filled_at["colsT",])
                    b = bank_of("colsT")
                    mcols = dtmp[:, 0:160]
                    again(V.tensor_copy(mcols, b[:, 0:160]))
                    V.tensor_copy(gcol[:, :, :], mcols[:, 0:32].rearrange("p (t h) -> p t h", h=4))
                    nm = mcols[:, 32:64].rearrange("p (t h) -> p t h", h=4)
                    mm = mcols[:, 64:96].rearrange("p (t h) -> p t h", h=4)
                    m_end = mcols[:, 96:128].rearrange("p (h t) -> p t h", h=4)
                    nM_end = mcols[:, 128:160].rearrange("p (h t) -> p t h", h=4)
                    V.tensor_copy(margs[:, 0, 0, :], nm[:, 0, :])
                    V.tensor_tensor(margs[:, 0, 1:T, :], nm[:, 1:T, :], m_end[:, 0:T - 1, :], ALU.add)
                    V.tensor_tensor(margs[:, 1, :, :], mcols[:, 0:32].rearrange("p (t h) -> p t h", h=4), nM_end, ALU.add)
                    V.tensor_copy(margs[:, 2, 0, :], nM_end[:, 0, :])
                    V.tensor_tensor(margs[:, 2, 1:T, :], nM_end[:, 1:T, :], m_end[:, 0:T - 1, :], ALU.add)
                    V.tensor_scalar(margs[:, 3, :, :], mm, -1.0, None, ALU.mult).then_inc(done, 1)
                elif k == "cols":
                    dve.wait_ge(filled, filled_at["apv", T - 1, 1, 1])
                    dve.wait_ge(vector_done["ano"], nth["ano", T - 1, 1, 1] + 1)
                    V.memset(raw[:, 0:3], 0.0)
                    for b in range(2):
                        V.memset(vm[b][0][:, :, M_DV + 1:VW].bitcast(F32), 0.0)
                        V.memset(vm[b][1][:, :, M_DV:VW].bitcast(F32), 0.0)
                    for b in range(2):
                        ins = V.memset(vm[b][0][:, :, M_DV:M_DV + 1].bitcast(F32), 1.0)
                    ins.then_inc(done, 1)
                elif k == "conv":
                    p, which = r
                    dve.wait_ge(scalar_done["mqkE"], nth["mqkE", p, which, 1] + 1)
                    if which:
                        dve.wait_ge(vector_done["qksp"], nth["qksp", p, 0] + 1)
                    elif p:
                        dve.wait_ge(filled, filled_at["kN", p - 1, T - 2])
                    w = cw[:, 2 * which + p, :]
                    again(V.tensor_scalar(cacc[:, :], raw[:, 0:S], w[:, 0:1], None, ALU.mult))
                    for t in range(1, CONV_K):
                        ins = V.scalar_tensor_tensor(out=cacc[:, :], in0=raw[:, t:t + S], scalar=w[:, t:t + 1],
                                                     in1=cacc[:, :], op0=ALU.mult, op1=ALU.add)
                        if t < CONV_K - 1:
                            again(ins)
                    ins.then_inc(done, 1)
                elif k == "qksp":
                    p, which = r
                    dve.wait_ge(scalar_done["silu"], nth["silu", p, which] + 1)
                    hi, lo = kmT if which else qmT
                    V.scalar_tensor_tensor(out=lo[:, :], in0=cacc[:, :], scalar=M_SCALE if which else 1.0,
                                           in1=hi[:, :].bitcast(F32), op0=ALU.mult, op1=ALU.subtract).then_inc(done, 1)
                elif k == "mSE":
                    p, i = r
                    dve.wait_ge(scalar_done["mBE"], nth["mBE", p, i] + 1)
                    dve.wait_ge(filled, filled_at["mS", p, i])
                    for j in range(2):
                        last = V.tensor_tensor(dtmp[:, j * P:(j + 1) * P], bank_of("mS", p, i, m=j)[:, 0:P],
                                               Wt[:, j, :], ALU.mult)
                    again(last)
                    if nth[step] >= 1:
                        dve.wait_ge(filled, filled_at["mO", *order_at["mSE", nth[step] - 1][1:]])
                    flat = lambda a: a[:, :, :].rearrange("p j t -> p (j t)")
                    again(V.tensor_copy(flat(sw[0]), dtmp[:, 0:2 * P]))
                    V.tensor_tensor(flat(sw[1]), dtmp[:, 0:2 * P], flat(sw[0]).bitcast(F32), ALU.subtract).then_inc(done, 1)
                elif k == "kNE":
                    p, i = r
                    dve.wait_ge(filled, filled_at["kN", p, i])
                    if i == 0 and p == 0:
                        dve.wait_ge(scalar_done["cols"], nth["cols",] + 1)
                    ws_ = margs[:, 1, i, 2 * p:2 * p + 2].unsqueeze(2).broadcast_to([P, 2, 64])
                    again(V.scalar_tensor_tensor(out=dtmp[:, 256:384].rearrange("p (j d) -> p j d", j=2),
                                                 in0=bank_of("kN", p, i)[:, 0:P].rearrange("p (j d) -> p j d", j=2),
                                                 scalar=M_SCALE, in1=ws_, op0=ALU.mult, op1=ALU.mult))
                    if nth[step] >= 1:
                        dve.wait_ge(filled, filled_at["mC", *order_at["kNE", nth[step] - 1][1:]])
                    again(V.tensor_copy(kw[0][:, :], dtmp[:, 256:384]))
                    V.tensor_tensor(kw[1][:, :], dtmp[:, 256:384], kw[0][:, :].bitcast(F32), ALU.subtract).then_inc(done, 1)
                elif k == "mOE":
                    p, i = r
                    dve.wait_ge(filled, filled_at["mO", p, i])
                    for j in range(2):
                        h = 2 * p + j
                        b = bank_of("mO", p, i, m=j)
                        y = rows[:, 0, i, M_DV * h:M_DV * (h + 1)]
                        if i:
                            V.tensor_copy(y, b[:, 0:M_DV])
                            again(V.tensor_copy(mden[:, i, h:h + 1], b[:, M_DV:M_DV + 1]))
                            V.scalar_tensor_tensor(out=y, in0=b[:, 256:256 + M_DV], scalar=margs[:, 0, i, h:h + 1],
                                                   in1=y, op0=ALU.mult, op1=ALU.add)
                            last = V.scalar_tensor_tensor(out=mden[:, i, h:h + 1], in0=b[:, 256 + M_DV:257 + M_DV],
                                                          scalar=margs[:, 0, i, h:h + 1], in1=mden[:, i, h:h + 1],
                                                          op0=ALU.mult, op1=ALU.add)
                        else:
                            V.tensor_copy(y, b[:, 0:M_DV])
                            last = V.tensor_copy(mden[:, i, h:h + 1], b[:, M_DV:M_DV + 1])
                    last.then_inc(done, 1)
                elif k == "mCE":
                    p, i = r
                    dve.wait_ge(filled, filled_at["mC", p, i])
                    b = bank_of("mC", p, i)
                    for j in range(2):
                        part = slice(64 * j, 64 * j + 64)
                        src = b[part, 256 * j:256 * j + VW]
                        if i == 0:
                            last = V.tensor_copy(Cst[part, :], src)
                        else:
                            last = V.scalar_tensor_tensor(out=Cst[part, :], in0=Cst[part, :],
                                                          scalar=margs[part, 2, i, 2 * p + j:2 * p + j + 1], in1=src,
                                                          op0=ALU.mult, op1=ALU.add)
                    again(last)
                    hi, lo = Csp[i % 2]
                    if i >= 2:
                        dve.wait_ge(filled, filled_at["mO", p, i - 1])
                    again(V.tensor_copy(hi[:, :], Cst[:, :]))
                    V.tensor_tensor(lo[:, :], Cst[:, :], hi[:, :].bitcast(F32), ALU.subtract).then_inc(done, 1)
                elif k == "mfin":
                    p = r[0]
                    dve.wait_ge(scalar_done["hsq"], nth["hsq", p, T - 1] + 1)
                    n = 2 * T
                    den, squares, scale_, floor = (a[:, :, 2 * p:2 * p + 2] for a in (mden, hss, msc_t, margs[:, 3]))
                    v, root = (nt[:, m, 0:n].rearrange("p (t h) -> p t h", h=2) for m in (0, 3))
                    again(V.scalar_tensor_tensor(out=den, in0=den, scalar=-1.0, in1=den, op0=ALU.mult, op1=ALU.max))
                    again(V.tensor_tensor(den, den, floor, ALU.max))
                    again(V.reciprocal(den, den))
                    again(V.tensor_tensor(squares, squares, den, ALU.mult))
                    again(V.tensor_tensor(squares, squares, den, ALU.mult))
                    again(V.tensor_scalar(v, squares, 1.0 / M_DV, EPS, ALU.mult, ALU.add))
                    inverse_root(nt[:, 3, 0:n], nt[:, 0, 0:n], n, None)
                    V.scalar_tensor_tensor(out=scale_, in0=root, scalar=0.5, in1=den, op0=ALU.mult, op1=ALU.mult)\
                        .then_inc(done, 1)
                    dve.wait_ge(vector_done[k], nth[step] + 1)
                elif k == "mscale":
                    p, i = r
                    for h in range(2 * p, 2 * p + 2):
                        y = rows[:, 0, i, M_DV * h:M_DV * (h + 1)]
                        last = V.scalar_tensor_tensor(out=y, in0=y, scalar=msc_t[:, i, h:h + 1],
                                                      in1=hg[:, M_DV * h:M_DV * (h + 1)], op0=ALU.mult, op1=ALU.mult)
                    last.then_inc(done, 1)
                elif k == "moE":
                    p, i = r
                    dve.wait_ge(scalar_done[k], nth[step] + 1)
                    dve.wait_ge(vector_done["mscale"], nth["mscale", p, i] + 1)
                    y = rows[:, 0, i, CW * p:CW * (p + 1)]
                    par = gate_no[step] % 2
                    V.scalar_tensor_tensor(out=y, in0=tmp[:, CW * par:CW * (par + 1)], scalar=1.0, in1=y,
                                           op0=ALU.add, op1=ALU.mult).then_inc(done, 1)
                elif k == "zE":
                    l, zc, i = r
                    if l == 1:
                        continue
                    dve.wait_ge(scalar_done[k], nth[step] + 1)
                    if zc < 2:
                        dve.wait_ge(vector_done["moE"], nth["moE", zc, i] + 1)
                    y = rows[:, zc // 2, i, CW * (zc % 2):CW * (zc % 2 + 1)]
                    par = gate_no[step] % 2
                    V.tensor_tensor(y, tmp[:, CW * par:CW * (par + 1)], y, ALU.mult).then_inc(done, 1)
                elif k == "poE":
                    l, oc, i = r
                    dve.wait_ge(filled, filled_at["po", l, oc, i])
                    if oc == 0:
                        dve.wait_ge(x_in[i], 16 * (l + 2))
                        dve.wait_ge(vector_done["adaE"], nth["adaE", l, 11] + 1)
                    t = dtmp[:, CW * (nth[step] % 2):CW * (nth[step] % 2 + 1)]
                    again(V.tensor_tensor(t, bank_of("po", l, oc, i)[:, 0:CW], gate_bc[:, CW * oc:CW * (oc + 1)], ALU.mult))
                    y = rows[:, oc // 2, i, CW * (oc % 2):CW * (oc % 2 + 1)]
                    V.tensor_tensor(y, y, t, ALU.add).then_inc(done, 1)
                elif k == "lrs":
                    dve.wait_ge(scalar_done["lsq"], nth["lsq", T - 1] + 1)
                    V.tensor_scalar(nt[:, 0, 0:T], ssq[:, 0:T], 1.0 / C_QL, EPS, ALU.mult, ALU.add)
                    again(V.tensor_scalar(nt[:, 0, T:2 * T], ssq[:, T:2 * T], 1.0 / C_KVL, EPS, ALU.mult, ALU.add))
                    inverse_root(rstd[:, 0:2 * T], nt[:, 0, 0:2 * T], 2 * T, done)
                    dve.wait_ge(vector_done[k], nth[step] + 1)
                elif k == "lsc":
                    i = r[0]
                    V.tensor_scalar(craw[:, i, 0:C_QL], craw[:, i, 0:C_QL], rstd[:, i:i + 1], None, ALU.mult)
                    V.tensor_scalar(craw[:, i, C_QL:O_KR], craw[:, i, C_QL:O_KR], rstd[:, T + i:T + i + 1], None, ALU.mult)
                    kr = craw[:, i:i + 1, O_KR:O_KR + 64]
                    again(rotate(craw[:, i:i + 1, O_KR + 64:CRW], kr, i, 1))
                    V.tensor_copy(kr, craw[:, i:i + 1, O_KR + 64:CRW]).then_inc(done, 1)
                elif k == "msm":
                    h, i = r
                    st = cst[:, nth[step] % 6, :]
                    n = i // 4 + 1
                    for b in range(n):
                        dve.wait_ge(filled, filled_at["msc", h, i, b])
                        nk = min(512, P * (i + 1) - 512 * b)
                        last = V.tensor_reduce(st[:, b:b + 1], bank_of("msc", h, i, b)[:, 0:nk], AX, ALU.max)
                    again(last)
                    if n == 2:
                        again(V.tensor_tensor(st[:, 0:1], st[:, 0:1], st[:, 1:2], ALU.max))
                    V.tensor_scalar(st[:, 2:3], st[:, 0:1], -C_SCALE, None, ALU.mult).then_inc(done, 1)
                elif k == "mno":
                    h, i = r
                    st = cst[:, nth["msm", h, i] % 6, :]
                    dve.wait_ge(scalar_done["mex"], nth["mex", h, i] + 1)
                    if i >= 4:
                        again(V.tensor_tensor(st[:, 3:4], st[:, 3:4], st[:, 4:5], ALU.add))
                    again(V.reciprocal(st[:, 5:6], st[:, 3:4]))
                    dve.wait_ge(filled, filled_at["mpv", h, i, i // 4])
                    if h % 2 == 0:
                        dve.wait_ge(scalar_done["zE"], nth["zE", 1, h // 2, i] + 1)
                    y = rows[:, h // 4, i, (h % 4) * P:(h % 4 + 1) * P]
                    b = bank[bank_no[job["mpv", h, i, 0]]]
                    again(V.tensor_copy(osum[:, :], b[:, P:2 * P]))
                    again(V.tensor_tensor(osum[:, :], b[:, 0:P], osum[:, :], ALU.add))
                    V.scalar_tensor_tensor(out=y, in0=osum[:, :], scalar=st[:, 5:6], in1=y,
                                           op0=ALU.mult, op1=ALU.mult).then_inc(done, 1)
                elif k == "fin":
                    i = r[1]
                    if i == 0:
                        dve.wait_ge(final_in, 16)
                    V.scalar_tensor_tensor(out=xhat[:, i, :].rearrange("p (a d) -> p a d", a=2), in0=rows[:, :, i, :],
                                           scalar=rstd[:, i:i + 1], in1=final_bc[:, :].rearrange("p (a d) -> p a d", a=2),
                                           op0=ALU.mult, op1=ALU.mult).then_inc(done, 1)
                else:
                    raise ValueError(k)


_INS = ["x", "ada_w", "ada_b", "e_w_in", "e_head_g", "e_sinks", "e_w_out", "o_w_in", "o_w_uq", "o_w_ukv", "o_w_out",
        "final_g"]


def constants():
    import numpy as np

    inv = np.float32(1.0) / (np.float32(10000.0) ** (np.arange(0, S_HD, 2, dtype=np.float32) / np.float32(S_HD)))
    ang = np.arange(S, dtype=np.float32)[:, None] * inv[None, :]
    cos, sin = np.cos(ang), np.sin(ang)
    rope = np.concatenate([cos, cos, -sin, sin], axis=1).astype(np.float32)
    small = np.zeros((P, 640), np.float32)
    big = -(2.0 ** 100)
    small[:, 0:128] = np.eye(P)
    small[:, 128:256] = np.where(np.arange(P)[:, None] <= np.arange(P)[None, :], 0.0, big)
    for at in (0, 64):
        small[at, 256:320] = 1.0
        small[at + 1, 320:384] = 1.0
        small[at, 384:448] = big
        small[at, 576:640] = big
        small[at + 1, 384:512] = big
    return {"rope": rope, "ident": np.eye(P, dtype=np.float32), "small": small}


def kernel(**inputs):
    import numpy as _np
    import concourse.bacc as _bacc
    from concourse import mybir as _mybir
    from concourse.bass_utils import run_bass_kernel_spmd as _run

    nc = _bacc.Bacc("TRN2", target_bir_lowering=False, num_devices=1)
    arrays, args = {}, []
    for name in _INS:
        arrays["in_" + name] = _np.ascontiguousarray(inputs[name])
    arrays["in_columns"] = _np.ascontiguousarray(_np.concatenate(
        [_np.asarray(inputs[n]).reshape(-1, P) for n in ("c", "norm_g", "e_conv_w", "o_q_g", "o_kv_g")]).T)
    arrays["in_gate_b"] = _np.ascontiguousarray(_np.asarray(inputs["e_gate_b"]).reshape(2, M_HEADS).T)
    for name, value in constants().items():
        arrays["const_" + name] = value
    for name, a in arrays.items():
        if name == "in_x":
            a = arrays[name] = a.reshape(S, D)
        args.append(nc.dram_tensor(name, a.shape, _mybir.dt.from_np(a.dtype), kind="ExternalInput").ap())
    args.append(nc.dram_tensor("out_0", (1, S, D), F32, kind="ExternalOutput").ap())
    trunk(nc, *args)
    r = _run(nc, [arrays], core_ids=[0])
    return r.results[0]["out_0"]
```
